# Optimizing a Trainium2 kernel written in Bass

```python
import math
import jax, jax.numpy as jnp
from jax import lax
import numpy as np

D_MODEL = 1024
BATCH = 1
SEQ = 256
DEPTH = 2

GRID_W = 64
CTX_LEN = 256
EPS = 1e-6
F32 = jnp.float32

SSD_HEADS = 8
SSD_HEAD_DIM = 64
SSD_INNER = SSD_HEADS * SSD_HEAD_DIM
SSD_GROUPS = 2
SSD_STATE = 128
SSD_CHUNK = 128
SSD_CONV = 3
SSD_GN = SSD_GROUPS * SSD_STATE
SSD_XB = SSD_INNER + SSD_GN
SSD_CONV_DIM = SSD_XB + SSD_GN

ATTN_HEADS = 8
ATTN_KV_HEADS = 2
ATTN_HEAD_DIM = 64
ATTN_Q_PER_KV = ATTN_HEADS // ATTN_KV_HEADS
ATTN_INNER = ATTN_HEADS * ATTN_HEAD_DIM
ATTN_KV_INNER = ATTN_KV_HEADS * ATTN_HEAD_DIM
ATTN_BLOCK = 128
ATTN_SCALE = ATTN_HEAD_DIM ** -0.5
ROPE_THETA = 10000.0
ROPE_AXIS_DIM = ATTN_HEAD_DIM // 2

HY_WIDTH = 512
HY_CONV = 3
HY_BANDS = 16
HY_EMB = 1 + 2 * HY_BANDS
HY_HIDDEN = 64
HY_FAST_DECAY_PCT = 0.3
HY_SLOW_DECAY_PCT = 1.5
HY_TARGET = 1e-2

D_MIX = SSD_INNER + ATTN_INNER + HY_WIDTH
D_FF = ((8 * D_MODEL // 3 + 255) // 256) * 256
N_MOD = 6

OFF_K = 0
OFF_V = OFF_K + ATTN_KV_INNER
OFF_XB = OFF_V + ATTN_KV_INNER
OFF_DT = OFF_XB + SSD_XB
CTX_STATE_COLS = OFF_DT + 2 * SSD_HEADS
OFF_C = CTX_STATE_COLS
OFF_Q = OFF_C + SSD_GN
OFF_Z = OFF_Q + ATTN_INNER
OFF_HY = OFF_Z + SSD_INNER
N_IN = OFF_HY + 3 * HY_WIDTH

kernel_name = 'hybrid_ssd_gqa_hyena_prefix_dit'

def _rmsnorm(t, g):
    tf = t.astype(F32)
    y = tf * lax.rsqrt(jnp.mean(tf * tf, axis=-1, keepdims=True) + EPS)
    return (y * g.astype(F32)).astype(t.dtype)

def _modulate(h, shift, scale):
    return h * (1.0 + scale) + shift

def _flip(t):
    return jnp.flip(t, axis=1)

def _dwconv(u, w, b):
    width, ch = w.shape
    pad = (width - 1) // 2
    y = lax.conv_general_dilated(u, w[:, None, :], window_strides=(1,), padding=[(pad, pad)],
                                 dimension_numbers=('NWC', 'WIO', 'NWC'), feature_group_count=ch)
    return y + b

def _segsum(a):
    T = a.shape[-1]
    cs = jnp.cumsum(a, axis=-1)
    diff = cs[..., :, None] - cs[..., None, :]
    mask = jnp.tril(jnp.ones((T, T), dtype=bool))
    return jnp.where(mask, diff, -jnp.inf)

def _heads_from_groups(t):
    b, L, _ = t.shape
    t = t.reshape(b, L, SSD_GROUPS, SSD_STATE)
    return jnp.repeat(t, SSD_HEADS // SSD_GROUPS, axis=2)

def _ssd_prep(proj, p):
    xb = jax.nn.silu(_dwconv(proj[..., OFF_XB:OFF_XB + SSD_XB],
                             p['ssd_conv_w'][:, :SSD_XB], p['ssd_conv_b'][:SSD_XB]))
    b, L, _ = xb.shape
    xs = xb[..., :SSD_INNER].reshape(b, L, SSD_HEADS, SSD_HEAD_DIM).astype(F32)
    bm = _heads_from_groups(xb[..., SSD_INNER:]).astype(F32)
    dt_raw = proj[..., OFF_DT:OFF_DT + 2 * SSD_HEADS].reshape(b, L, 2, SSD_HEADS).astype(F32)
    dt = jax.nn.softplus(dt_raw + p['ssd_dt_bias'].astype(F32))
    return xs, bm, dt

def _ssd_cproj(proj, p):
    cm = jax.nn.silu(_dwconv(proj[..., OFF_C:OFF_C + SSD_GN],
                             p['ssd_conv_w'][:, SSD_XB:], p['ssd_conv_b'][SSD_XB:]))
    return _heads_from_groups(cm).astype(F32)

def _ssd_scan(xs, dt, a, bm, cm, init):
    b, L, H, P = xs.shape
    nc = L // SSD_CHUNK
    X = (xs * dt[..., None]).reshape(b, nc, SSD_CHUNK, H, P)
    Bc = bm.reshape(b, nc, SSD_CHUNK, H, SSD_STATE)
    Cc = cm.reshape(b, nc, SSD_CHUNK, H, SSD_STATE)
    a_dt = (dt * a).reshape(b, nc, SSD_CHUNK, H).transpose(0, 3, 1, 2)
    a_cs = jnp.cumsum(a_dt, axis=-1)
    scores = jnp.einsum('bclhn,bcshn->bhcls', Cc, Bc) * jnp.exp(_segsum(a_dt))
    y_diag = jnp.einsum('bhcls,bcshp->bclhp', scores, X)
    decay_states = jnp.exp(a_cs[..., -1:] - a_cs)
    states = jnp.einsum('bclhn,bhcl,bclhp->bchpn', Bc, decay_states, X)
    states = jnp.concatenate([init[:, None], states], axis=1)
    chunk_decay = jnp.exp(_segsum(jnp.pad(a_cs[..., -1], ((0, 0), (0, 0), (1, 0)))))
    states = jnp.einsum('bhzc,bchpn->bzhpn', chunk_decay, states)
    y_off = jnp.einsum('bclhn,bchpn,bhcl->bclhp', Cc, states[:, :-1], jnp.exp(a_cs))
    return (y_diag + y_off).reshape(b, L, H, P), states[:, -1]

def _ssd_final_state(xs, dt, a, bm):
    cs = jnp.cumsum(dt * a, axis=1)
    w = jnp.exp(cs[:, -1:] - cs) * dt
    return jnp.einsum('blhn,blh,blhp->bhpn', bm, w, xs)

def _ssd_out(y, xs, z, p):
    b, L = y.shape[:2]
    y = (y + p['ssd_d'].astype(F32)[:, None] * xs).reshape(b, L, SSD_INNER)
    y = y * jax.nn.silu(z.astype(F32))
    return _rmsnorm(y, p['ssd_norm_g']).astype(z.dtype)

def _ssd_mixer(proj, projc, p, last):
    a = -jnp.exp(p['ssd_a_log'].astype(F32))
    xs, bm, dt = _ssd_prep(proj, p)
    cm = _ssd_cproj(proj, p)
    xs_c, bm_c, dt_c = _ssd_prep(projc, p)
    if last:
        s_f = _ssd_final_state(xs_c, dt_c[:, :, 0], a[0], bm_c)
        s_b = _ssd_final_state(_flip(xs_c), _flip(dt_c[:, :, 1]), a[1], _flip(bm_c))
        y_c = None
    else:
        cm_c = _ssd_cproj(projc, p)
        zeros = jnp.zeros((xs_c.shape[0], SSD_HEADS, SSD_HEAD_DIM, SSD_STATE), F32)
        yc_f, s_f = _ssd_scan(xs_c, dt_c[:, :, 0], a[0], bm_c, cm_c, zeros)
        yc_b, s_b = _ssd_scan(_flip(xs_c), _flip(dt_c[:, :, 1]), a[1], _flip(bm_c), _flip(cm_c), zeros)
        y_c = _ssd_out(yc_f + _flip(yc_b), xs_c, projc[..., OFF_Z:OFF_Z + SSD_INNER], p)
    y_f, _ = _ssd_scan(xs, dt[:, :, 0], a[0], bm, cm, s_f)
    y_b, _ = _ssd_scan(_flip(xs), _flip(dt[:, :, 1]), a[1], _flip(bm), _flip(cm), s_b)
    y = _ssd_out(y_f + _flip(y_b), xs, proj[..., OFF_Z:OFF_Z + SSD_INNER], p)
    return y, y_c

def _rope_half(t, cos, sin):
    t1, t2 = jnp.split(t, 2, axis=-1)
    return jnp.concatenate([t1 * cos - t2 * sin, t2 * cos + t1 * sin], axis=-1)

def _rope2d(t, rope):
    cos_r, sin_r, cos_c, sin_c = rope
    tr, tc = jnp.split(t.astype(F32), 2, axis=-1)
    out = jnp.concatenate([_rope_half(tr, cos_r[:, None], sin_r[:, None]),
                           _rope_half(tc, cos_c[:, None], sin_c[:, None])], axis=-1)
    return out.astype(t.dtype)

def _gqa(q, k, v):
    s = jnp.einsum('bqgrd,bkgd->bgrqk', q, k).astype(F32)
    pr = jax.nn.softmax(s, axis=-1).astype(v.dtype)
    return jnp.einsum('bgrqk,bkgd->bqgrd', pr, v)

def _split_heads(t, n):
    return t.reshape(t.shape[0], t.shape[1], n, ATTN_HEAD_DIM)

def _attn_mixer(proj, projc, p, rope, last):
    b, L, _ = proj.shape
    q = _rope2d(_rmsnorm(_split_heads(proj[..., OFF_Q:OFF_Q + ATTN_INNER], ATTN_HEADS), p['q_norm_g']), rope) * ATTN_SCALE
    k = _rope2d(_rmsnorm(_split_heads(proj[..., OFF_K:OFF_K + ATTN_KV_INNER], ATTN_KV_HEADS), p['k_norm_g']), rope)
    v = _split_heads(proj[..., OFF_V:OFF_V + ATTN_KV_INNER], ATTN_KV_HEADS)
    kc = _rmsnorm(_split_heads(projc[..., OFF_K:OFF_K + ATTN_KV_INNER], ATTN_KV_HEADS), p['k_norm_g'])
    vc = _split_heads(projc[..., OFF_V:OFF_V + ATTN_KV_INNER], ATTN_KV_HEADS)
    k_all = jnp.concatenate([kc, k], axis=1)
    v_all = jnp.concatenate([vc, v], axis=1)
    nb = L // ATTN_BLOCK
    q_blocks = q.reshape(b, nb, ATTN_BLOCK, ATTN_KV_HEADS, ATTN_Q_PER_KV, ATTN_HEAD_DIM).transpose(1, 0, 2, 3, 4, 5)
    o = lax.map(lambda qb: _gqa(qb, k_all, v_all), q_blocks)
    y = _rmsnorm(o.transpose(1, 0, 2, 3, 4, 5).reshape(b, L, ATTN_INNER), p['attn_norm_g'])
    if last:
        return y, None
    bc, lc, _ = projc.shape
    qc = _rmsnorm(_split_heads(projc[..., OFF_Q:OFF_Q + ATTN_INNER], ATTN_HEADS), p['q_norm_g']) * ATTN_SCALE
    oc = _gqa(qc.reshape(bc, lc, ATTN_KV_HEADS, ATTN_Q_PER_KV, ATTN_HEAD_DIM), kc, vc)
    y_c = _rmsnorm(oc.reshape(bc, lc, ATTN_INNER), p['attn_norm_g'])
    return y, y_c

def _hyena_filter(L, p):
    t = jnp.linspace(0.0, 1.0, L, dtype=F32)[:, None]
    w = 2.0 * math.pi * jnp.arange(L, dtype=F32)[:, None] / L
    f = jnp.linspace(1e-4, HY_BANDS - 1, HY_BANDS, dtype=F32)
    feats = jnp.concatenate([t, jnp.cos(f * w), -jnp.sin(f * w)], axis=-1)
    freq = p['hy_freq'].astype(F32)
    hdn = jnp.sin(freq * (feats @ p['hy_w1'].astype(F32) + p['hy_b1'].astype(F32)))
    hdn = jnp.sin(freq * (hdn @ p['hy_w2'].astype(F32) + p['hy_b2'].astype(F32)))
    filt = (hdn @ p['hy_w3'].astype(F32)).reshape(L, 2, HY_WIDTH)
    max_decay = math.log(HY_TARGET) / HY_FAST_DECAY_PCT
    min_decay = math.log(HY_TARGET) / HY_SLOW_DECAY_PCT
    deltas = jnp.linspace(min_decay, max_decay, HY_WIDTH, dtype=F32)
    decay = jnp.exp(-t * jnp.abs(deltas))
    return filt * decay[:, None, :]

def _long_conv(u, filt, bias):
    L = u.shape[1]
    taps = jnp.concatenate([filt[:, 0], jnp.zeros((1, HY_WIDTH), F32), filt[:0:-1, 1]], axis=0)
    kf = jnp.fft.rfft(taps, n=2 * L, axis=0)
    uf = jnp.fft.rfft(u, n=2 * L, axis=1)
    y = jnp.fft.irfft(uf * kf[None], n=2 * L, axis=1)[:, :L]
    return y + u * bias

def _hyena_mixer(u_raw, p):
    u = _dwconv(u_raw, p['hy_conv_w'], p['hy_conv_b']).astype(F32)
    v, x1, x0 = jnp.split(u, 3, axis=-1)
    filt = _hyena_filter(u.shape[1], p)
    y = x0 * _long_conv(v * x1, filt, p['hy_bias'].astype(F32))
    return _rmsnorm(y, p['hy_norm_g']).astype(u_raw.dtype)

def _swiglu(h, p):
    gate, up = jnp.split(h @ p['w_gu'], 2, axis=-1)
    return (jax.nn.silu(gate) * up) @ p['w_down']

def _layer(x, xc, c_act, cctx_act, p, rope, last):
    mod = (c_act @ p['w_mod'] + p['b_mod'])[:, None, :]
    sh1, sc1, g1, sh2, sc2, g2 = jnp.split(mod, N_MOD, axis=-1)
    n_ctx_mod = 2 if last else N_MOD
    mod_c = cctx_act @ p['w_mod'][:, :n_ctx_mod * D_MODEL] + p['b_mod'][:n_ctx_mod * D_MODEL]
    mod_c = jnp.split(mod_c, n_ctx_mod)
    h = _modulate(_rmsnorm(x, p['norm1_g']), sh1, sc1)
    hc = _modulate(_rmsnorm(xc, p['norm1_g']), mod_c[0], mod_c[1])
    proj = h @ p['w_in']
    n_ctx_cols = CTX_STATE_COLS if last else N_IN
    projc = hc @ p['w_in'][:, :n_ctx_cols]
    y_ssd, y_ssd_c = _ssd_mixer(proj, projc, p, last)
    y_att, y_att_c = _attn_mixer(proj, projc, p, rope, last)
    y_hy = _hyena_mixer(proj[..., OFF_HY:], p)
    x = x + g1 * (jnp.concatenate([y_ssd, y_att, y_hy], axis=-1) @ p['w_out'])
    x = x + g2 * _swiglu(_modulate(_rmsnorm(x, p['norm2_g']), sh2, sc2), p)
    if last:
        return x, None
    y_hy_c = _hyena_mixer(projc[..., OFF_HY:], p)
    xc = xc + mod_c[2] * (jnp.concatenate([y_ssd_c, y_att_c, y_hy_c], axis=-1) @ p['w_out'])
    xc = xc + mod_c[5] * _swiglu(_modulate(_rmsnorm(xc, p['norm2_g']), mod_c[3], mod_c[4]), p)
    return x, xc

def setup_inputs(seed: int = 0) -> dict:
    key = jax.random.key(seed)
    ks = jax.random.split(key, 40)

    def nrm(k, shape, scale):
        return jax.random.normal(k, shape, F32) * scale

    def gain(k, shape):
        return 1.0 + 0.05 * jax.random.normal(k, shape, F32)

    dt0 = jnp.exp(jax.random.uniform(ks[10], (DEPTH, 2, SSD_HEADS), F32, math.log(1e-3), math.log(1e-1)))
    return {
        'x': nrm(ks[0], (BATCH, SEQ, D_MODEL), 1.0),
        'c': nrm(ks[1], (BATCH, D_MODEL), 1.0),
        'ctx': nrm(ks[2], (BATCH, CTX_LEN, D_MODEL), 1.0),
        'c_ctx': nrm(ks[3], (D_MODEL,), 1.0),
        'w_mod': nrm(ks[4], (DEPTH, D_MODEL, N_MOD * D_MODEL), 0.5 * D_MODEL ** -0.5),
        'b_mod': nrm(ks[5], (DEPTH, N_MOD * D_MODEL), 0.02),
        'norm1_g': gain(ks[6], (DEPTH, D_MODEL)),
        'w_in': nrm(ks[7], (DEPTH, D_MODEL, N_IN), D_MODEL ** -0.5),
        'ssd_conv_w': nrm(ks[8], (DEPTH, SSD_CONV, SSD_CONV_DIM), SSD_CONV ** -0.5),
        'ssd_conv_b': nrm(ks[9], (DEPTH, SSD_CONV_DIM), 0.02),
        'ssd_a_log': jnp.log(jax.random.uniform(ks[11], (DEPTH, 2, SSD_HEADS), F32, 1.0, 16.0)),
        'ssd_dt_bias': dt0 + jnp.log(-jnp.expm1(-dt0)),
        'ssd_d': 1.0 + 0.1 * jax.random.normal(ks[12], (DEPTH, SSD_HEADS), F32),
        'ssd_norm_g': gain(ks[13], (DEPTH, SSD_INNER)),
        'q_norm_g': gain(ks[14], (DEPTH, ATTN_HEAD_DIM)),
        'k_norm_g': gain(ks[15], (DEPTH, ATTN_HEAD_DIM)),
        'attn_norm_g': gain(ks[16], (DEPTH, ATTN_INNER)),
        'hy_conv_w': nrm(ks[17], (DEPTH, HY_CONV, 3 * HY_WIDTH), HY_CONV ** -0.5),
        'hy_conv_b': nrm(ks[18], (DEPTH, 3 * HY_WIDTH), 0.02),
        'hy_w1': nrm(ks[19], (DEPTH, HY_EMB, HY_HIDDEN), HY_EMB ** -0.5),
        'hy_b1': nrm(ks[20], (DEPTH, HY_HIDDEN), 0.02),
        'hy_freq': gain(ks[21], (DEPTH, HY_HIDDEN)),
        'hy_w2': nrm(ks[22], (DEPTH, HY_HIDDEN, HY_HIDDEN), HY_HIDDEN ** -0.5),
        'hy_b2': nrm(ks[23], (DEPTH, HY_HIDDEN), 0.02),
        'hy_w3': nrm(ks[24], (DEPTH, HY_HIDDEN, 2 * HY_WIDTH), HY_HIDDEN ** -0.5),
        'hy_bias': nrm(ks[25], (DEPTH, HY_WIDTH), 1.0),
        'hy_norm_g': gain(ks[26], (DEPTH, HY_WIDTH)),
        'w_out': nrm(ks[27], (DEPTH, D_MIX, D_MODEL), D_MIX ** -0.5),
        'norm2_g': gain(ks[28], (DEPTH, D_MODEL)),
        'w_gu': nrm(ks[29], (DEPTH, D_MODEL, 2 * D_FF), D_MODEL ** -0.5),
        'w_down': nrm(ks[30], (DEPTH, D_FF, D_MODEL), D_FF ** -0.5),
        'final_g': gain(ks[31], (D_MODEL,)),
    }

def reference(x, c, ctx, c_ctx, w_mod, b_mod, norm1_g, w_in, ssd_conv_w, ssd_conv_b, ssd_a_log,
              ssd_dt_bias, ssd_d, ssd_norm_g, q_norm_g, k_norm_g, attn_norm_g, hy_conv_w, hy_conv_b,
              hy_w1, hy_b1, hy_freq, hy_w2, hy_b2, hy_w3, hy_bias, hy_norm_g, w_out, norm2_g, w_gu,
              w_down, final_g):
    L = x.shape[1]
    ROWS = L // GRID_W
    row = jnp.repeat(jnp.arange(ROWS, dtype=F32), GRID_W)
    col = jnp.tile(jnp.arange(GRID_W, dtype=F32), ROWS)
    inv_freq = ROPE_THETA ** (-jnp.arange(0, ROPE_AXIS_DIM, 2, dtype=F32) / ROPE_AXIS_DIM)
    ang_r = row[:, None] * inv_freq
    ang_c = col[:, None] * inv_freq
    rope = (jnp.cos(ang_r), jnp.sin(ang_r), jnp.cos(ang_c), jnp.sin(ang_c))
    c_act = jax.nn.silu(c)
    cctx_act = jax.nn.silu(c_ctx)
    xc = ctx
    for l in range(DEPTH):
        p = {
            'w_mod': w_mod[l], 'b_mod': b_mod[l], 'norm1_g': norm1_g[l], 'w_in': w_in[l],
            'ssd_conv_w': ssd_conv_w[l], 'ssd_conv_b': ssd_conv_b[l], 'ssd_a_log': ssd_a_log[l],
            'ssd_dt_bias': ssd_dt_bias[l], 'ssd_d': ssd_d[l], 'ssd_norm_g': ssd_norm_g[l],
            'q_norm_g': q_norm_g[l], 'k_norm_g': k_norm_g[l], 'attn_norm_g': attn_norm_g[l],
            'hy_conv_w': hy_conv_w[l], 'hy_conv_b': hy_conv_b[l], 'hy_w1': hy_w1[l], 'hy_b1': hy_b1[l],
            'hy_freq': hy_freq[l], 'hy_w2': hy_w2[l], 'hy_b2': hy_b2[l], 'hy_w3': hy_w3[l],
            'hy_bias': hy_bias[l], 'hy_norm_g': hy_norm_g[l], 'w_out': w_out[l], 'norm2_g': norm2_g[l],
            'w_gu': w_gu[l], 'w_down': w_down[l],
        }
        x, xc = _layer(x, xc, c_act, cctx_act, p, rope, l == DEPTH - 1)
    return _rmsnorm(x, final_g)


_drawn_inputs = setup_inputs


def setup_inputs(seed=0):
    import zlib

    import numpy as np

    out = dict(_drawn_inputs(seed))
    spreads = {}
    factors = {'ssd_conv_b': 7.858,
     'ssd_d': 5.752,
     'ssd_norm_g': 4.721,
     'q_norm_g': 8.0,
     'k_norm_g': 8.0,
     'attn_norm_g': 4.113,
     'hy_conv_b': 6.718,
     'hy_b1': 7.531,
     'hy_freq': 5.053,
     'hy_b2': 5.157,
     'hy_norm_g': 4.346}
    for name, (base, spread) in spreads.items():
        noise = np.random.default_rng([zlib.crc32(name.encode()), seed]).standard_normal(out[name].shape)
        drawn = base * np.exp(spread * noise) if base else spread * noise
        out[name] = __import__('jax').numpy.asarray(drawn.astype(out[name].dtype))
    for name, factor in factors.items():
        out[name] = (out[name] * factor).astype(out[name].dtype)
    return out
```

```python
import numpy as np
import concourse.bass as bass
from concourse import mybir
from contextlib import ExitStack

F32 = mybir.dt.float32
F32R = mybir.dt.float32r
ACT = mybir.ActivationFunctionType
ALU = mybir.AluOpType
AX_X = mybir.AxisListType.X

P = 128
D = 1024
L = 256
T = 2 * L
DEPTH = 2
KD = D // P
EPS = 1e-6
HEADS, HD = 8, 64
QKW = (HEADS + 2) * HD
GN = 256
NFREQ = 4
DFF = 2816
MODB = 6 * KD
CW = 256
OFF_K, OFF_XB, OFF_DT, OFF_C, OFF_Q, OFF_Z, OFF_HY = 0, 256, 1024, 1040, 1296, 1808, 2320

V_BMOD, V_N1, V_N2, V_SSDG, V_ATTG, V_HYG, V_SCB, V_HCB, V_FIN = 0, 48, 56, 64, 68, 72, 76, 84, 96
NA = 104
V_SCW, V_HCW, V_C, V_CC = NA, NA + 24, NA + 60, NA + 68
NB = 76
NV = NA + NB

W_IN = ([("xbc", OFF_XB + CW * i, i) for i in range(3)] + [("xbc", OFF_C, 3)]
        + [("z", OFF_Z + CW * i, i) for i in range(2)] + [("kv", OFF_K, 0)]
        + [("q", OFF_Q + CW * i, i) for i in range(2)]
        + [("hy", OFF_HY + CW * i, i) for i in range(6)])
FFN = [(0, 6), (6, 5)]

STAGES = [("in", 15, 15), ("out", 8, 4), ("gu0", 12, 12), ("down0", 8, 4), ("gu1", 10, 10), ("down1", 8, 4)]


def plan():
    at, g, q = {}, 0, 0
    for l in range(DEPTH):
        for name, chunks, pairs in STAGES:
            at[l, name] = (g, q)
            g, q = g + chunks, q + pairs
    return at


PLAN = plan()
LAST_CHUNK = PLAN[DEPTH - 1, "down1"][0] + 7
HALF = 4 * CW
SMALL_LOADS = 48
CONV_CHUNKS = sum(kind in ("xbc", "hy") for kind, _, _ in W_IN)
CONV_BANK = (5, 6, 7, 0)
MODS = DEPTH * MODB // 2
MODS_BEFORE, MODS_IN = 11, 15
PV_BEFORE = (0, 8 * T // P)


def ffn_at(l, part):
    return l * sum(n for _, n in FFN) + sum(n for _, n in FFN[:part])


def constants():
    f4 = np.float32
    i = np.arange(P)
    sq = np.zeros((P, 6, P), f4)
    sq[:, 0] = np.eye(P)
    sq[:, 1] = 1.0
    sq[:, 2] = i[:, None] <= i[None, :]
    sq[:, 3] = i[:, None] >= i[None, :]
    sq[:, 4] = np.where(i[:, None] <= i[None, :], 0.0, -1e30)
    sq[:, 5] = np.where(i[:, None] >= i[None, :], 0.0, -1e30)
    t = np.arange(L)[:, None].astype(np.float64)
    k = np.arange(L)[None, :].astype(np.float64)
    cos, sin = np.cos(2 * np.pi * k * t / (2 * L)), np.sin(2 * np.pi * k * t / (2 * L))
    alt = (-1.0) ** t
    fwd = np.concatenate([cos, alt, sin[:, 1:], 0 * alt, sin[:, 1:P], alt, cos[:, 1:P]], axis=1)
    fwd = fwd.reshape(2, P, 6 * P).transpose(1, 0, 2)
    w = np.where(k == 0, 1.0, 2.0)
    inv = np.concatenate([(cos * w).T, alt.T, 2 * sin[:, 1:].T], axis=0) / (2 * L)
    inv = inv.reshape(NFREQ, P, L).transpose(1, 0, 2)
    tl = np.linspace(0.0, 1.0, L, dtype=f4)[:, None]
    wl = (2.0 * np.pi * np.arange(L) / L).astype(f4)[:, None]
    fl = np.linspace(1e-4, 15, 16, dtype=f4)
    arg = (fl * wl).astype(f4).astype(np.float64)
    feats = np.concatenate([tl, np.cos(arg), -np.sin(arg)], axis=-1).T
    deltas = np.linspace(np.log(1e-2) / 1.5, np.log(1e-2) / 0.3, 512, dtype=f4)
    decay = np.exp((-tl * np.abs(deltas)).astype(f4).astype(np.float64)).reshape(2, P, 512).transpose(1, 0, 2)
    freq = (10000.0 ** (-np.arange(0, 32, 2) / 32)).astype(f4)
    row, col = np.repeat(np.arange(L // 64), 64).astype(f4), np.tile(np.arange(64), L // 64).astype(f4)
    ar, ac = (row[:, None] * freq).astype(np.float64), (col[:, None] * freq).astype(np.float64)
    rc = np.concatenate([np.cos(ar), np.cos(ar), np.cos(ac), np.cos(ac)], axis=1)
    rs = np.concatenate([-np.sin(ar), np.sin(ar), -np.sin(ac), np.sin(ac)], axis=1)
    rope = np.stack([rc, rs]).reshape(2, 2, P, 64).transpose(2, 0, 1, 3)
    return {"sq": sq, "fwd": fwd, "inv": inv, "feats": feats, "decay": decay, "rope": rope}


def backbone(nc, x, c, ctx_in, c_ctx, w_mod, b_mod, norm1_g, w_in, ssd_conv_w, ssd_conv_b, ssd_a_log,
             ssd_dt_bias, ssd_d, ssd_norm_g, q_norm_g, k_norm_g, attn_norm_g, hy_conv_w, hy_conv_b,
             hy_w1, hy_b1, hy_freq, hy_w2, hy_b2, hy_w3, hy_bias, hy_norm_g, w_out, norm2_g, w_gu,
             w_down, final_g, k_sq, k_fwd, k_inv, k_feats, k_decay, k_rope, out):
    with ExitStack() as stack:
        base = (nc.sbuf_base + 63) // 64 * 64
        KB = 1024

        def at(name, kb, shape, dt=F32):
            return nc.alloc_sbuf_tensor_at(name, [P] + shape, dt, offset=base + int(kb * KB))

        def sem(name):
            return stack.enter_context(nc.semaphore(name))

        xT = at("xT", 0, [KD, T])
        h_hi, h_lo = at("h_hi", 16, [KD, T], F32R), at("h_lo", 32, [KD, T], F32R)
        f_hi, f_lo = at("f_hi", 48, [12, T], F32R), at("f_lo", 72, [12, T], F32R)
        w_raw = at("w_raw", 96, [2, 8 * CW])
        w_hi, w_lo = at("w_hi", 112, [2, 8 * CW], F32R), at("w_lo", 128, [2, 8 * CW], F32R)
        m_raw = at("m_raw", 144, [2, 8 * CW])
        qk = at("qk", 160, [4, QKW])
        v_nat = at("v_nat", 170, [4, 2 * HD])
        spec = at("spec", 172, [5, 512])
        csT = at("csT", 182, [T])
        gate = at("gate", 160, [2, T])
        hidden = at("hidden", 164, [2, T])
        c_sq = at("c_sq", 184, [6, P])
        c_fwd = at("c_fwd", 187, [2, 6 * P])
        c_inv = at("c_inv", 193, [NFREQ, L])
        c_rope = at("c_rope", 197, [2, 2, HD])
        vecT = at("vecT", 198, [DEPTH, NV])
        modv = at("modv", 199.5, [DEPTH, MODB, 2])
        amod = at("amod", 200.25, [DEPTH, 2, KD, 2])
        qkg = at("qkg", 200.5, [DEPTH, 2, HD])
        wdt = at("wdt", 201.5, [8, 16])
        wdt_hi, wdt_lo = at("wdt_hi", 202, [8, 16], F32R), at("wdt_lo", 202.5, [8, 16], F32R)
        bc16 = at("bc16", 203, [DEPTH, 3, 16])
        cact = at("cact", 203.5, [KD, 2])
        hyc = at("hyc", 203.625, [4])
        (dtr, dab, dmx, dt, adt, cs, ncs, tot, wst, ecs, etot) = (
            at(n, 203.75 + 0.25 * i, [4, 16]) for i, n in enumerate(
                ("dtr", "dab", "dmx", "dt", "adt", "cs", "ncs", "tot", "wst", "ecs", "etot")))
        st4 = at("st4", 206.5, [4])
        sm = at("sm", 206.5625, [3, 16])
        rs40 = at("rs40", 206.8125, [4, 10])
        eps1 = at("eps1", 207, [1])
        t_w1, t_w2, t_w3 = at("t_w1", 48, [HD]), at("t_w2", 48.25, [HD]), at("t_w3", 48.5, [D])
        t_arg, t_k, t_h = at("t_arg", 52.5, [L]), at("t_k", 53.5, [L]), at("t_h", 54.5, [2, L])
        t_filt = at("t_filt", 57, [2, D])
        t_feats, t_decay = at("t_feats", 72, [L]), at("t_decay", 73, [2, 512])
        t_sum, t_diff = at("t_sum", 77, [2, 512]), at("t_diff", 81, [2, 512])
        t_hyb = at("t_hyb", 85, [512])
        sqr, hf = at("sqr", 48, [2, T]), at("hf", 52, [2, T])
        hm, rstd = at("hm", 56, [2, T]), at("rstd", 60, [T])
        lnt = at("lnt", 62, [T])
        x_nat = at("x_nat", 16, [4, D])
        stag = at("stag", 32, [DEPTH, 2, P])
        y_nat = at("y_nat", 16, [2, D])
        y_fin = at("y_fin", 32, [KD, L])
        xbc = at("xbc", 48, [8, T])
        x0 = at("x0", 64, [4, T])
        zs = at("zs", 72, [4, 512])
        x1 = at("x1", 80, [4, T])
        hyv = at("hyv", 88, [4, T])
        gT = at("gT", 80, [2, 4, P])
        bnat = at("bnat", 84, [4, GN])
        xsn = at("xsn", 16, [4, 512])
        ysum = at("ysum", 24, [4, 512])
        mt = at("mt", 32, [4, T])
        em = at("em", 40, [2, T])
        xw, state = at("xw", 44, [512]), at("state", 46, [512])
        prob, probT = at("prob", 16, [2, T]), at("probT", 20, [2, T])
        qT, kT = at("qT", 24, [4, T]), at("kT", 32, [T])
        onat = at("onat", 34, [4, 512])
        qkn, ropt = at("qkn", 42, [QKW]), at("ropt", 45, [QKW])
        vn = at("vn", 16, [4, 512])
        yspec = at("yspec", 24, [NFREQ, 512])
        prod = at("prod", 32, [2, 512])
        yhy = at("yhy", 36, [4, T])
        hsq = at("hsq", 44, [T])
        hrs = at("hrs", 46, [T])

        ps = stack.enter_context(nc.psum_tensor("ps", [P, 8, 512], F32))
        MOD, STAT = 4, 5
        ident, ones, trif, trib = (c_sq[:, i, :] for i in range(4))

        w_full = [sem("w_full0"), sem("w_full1")]
        w_hi_done = sem("w_hi_done")
        w_lo_pool, w_lo_dve = sem("w_lo_pool"), sem("w_lo_dve")
        w_used = sem("w_used")
        pair_free = [sem("pair_free0"), sem("pair_free1")]
        m_full = [sem("m_full0"), sem("m_full1")]
        mod_done = sem("mod_done")
        consts_full, x_full, small_full, hyw_full = sem("consts_full"), sem("x_full"), sem("small_full"), sem("hyw_full")
        wdt_full, wdt_hi_done, wdt_split = sem("wdt_full"), sem("wdt_hi_done"), sem("wdt_split")
        out_stored = sem("out_stored")
        conv_init = sem("conv_init")
        ffn_hi, ffn_lo = sem("ffn_hi"), sem("ffn_lo")
        reached = {e: sem(f"{e}_reached") for e in ("pe", "act", "dve")}
        S = {name: sem(name) for name in (
            "x_transposed", "xT_ready", "vec_transposed", "cact_ready",
            "filt_psum", "arg_ready", "sine_ready", "taps_ready", "spectra_psum",
            "squares", "square_summed", "rstd_ready", "hm_ready", "h_hi_ready", "h_ready", "dt_psum",
            "dt_abs", "softplus_tail", "adt_ready", "cums_psum", "decays_arg", "xs_transposed", "xsn_ready",
            "bnat_ready", "g_cst_psum", "g_cst_ready", "cum_rows", "diff_ready", "decay_exp", "mt_ready",
            "y_head_done", "state_ready", "yoff_psum", "xw_ready", "state_psum", "y_gated", "y_rms", "y_normed",
            "feat_psum", "f_hi_ready",
            "head_ss", "head_rms", "heads_ready", "heads_transposed", "qkT_ready", "scores", "row_max",
            "probs_ready", "probT_psum", "probT_ready", "pv_done", "o_ready", "o_rms", "o_normed",
            "vx_transposed", "vn_ready", "spec_psum", "yspec_ready", "conv_psum", "yhy_part",
            "hy_sq", "hy_summed", "hy_rms", "yhy_normed", "y_fin_ready", "y_fin_psum", "y_nat_ready",
            "dve_link", "act_link")}

        class Program:

            def __init__(self, eng, me):
                self.eng, self.me = eng, me
                self.made, self.seen, self.points = {}, {}, 0

            def sig(self, ins, name):
                self.made[name] = self.made.get(name, 0) + 1
                ins.then_inc(S[name], 1)

            def after(self, name, k=1):
                self.seen[name] = self.seen.get(name, 0) + k
                self.eng.wait_ge(S[name], self.seen[name])

            def own(self, name):
                self.eng.wait_ge(S[name], self.made[name])

            def link(self, ins):
                self.sig(ins, f"{self.me}_link")

            def settle(self):
                self.own(f"{self.me}_link")

            def chain(self, ins):
                self.link(ins)
                self.settle()

            def barrier(self):
                self.points += 1
                self.eng.drain().then_inc(reached[self.me], 1)
                for e in ("pe", "act", "dve"):
                    if e != self.me:
                        self.eng.wait_ge(reached[e], self.points)

        def tokens(l):
            return T if l == 0 else L

        def tile_orders(d):
            return (2, 3, 0, 1) if d == 0 else (3, 2, 1, 0)

        def per_head(src, t, d):
            return src[:, t, 8 * d:8 * d + 8].unsqueeze(2).to_broadcast([P, 8, HD])

        def heads(ap):
            return ap.rearrange("p (h d) -> p h d", d=HD)

        block = stack.enter_context(nc.Block())

        @block.sync
        def _(sp):
            sp.dma_start(x_nat[:, 0:2, :], x[0].rearrange("(t p) d -> p t d", p=P)).then_inc(x_full, 16)
            sp.dma_start(x_nat[:, 2:4, :], ctx_in[0].rearrange("(t p) d -> p t d", p=P)).then_inc(x_full, 16)
            for dst, src in ((c_sq, k_sq), (c_fwd, k_fwd), (c_inv, k_inv), (c_rope, k_rope)):
                sp.dma_start(dst[:], src).then_inc(consts_full, 16)

            def load_mod(m, i=0):
                if m >= 2:
                    sp.wait_ge(mod_done, i * 2 + (m - 1))
                src = w_mod[m // 24].rearrange("(k p) n -> p k n", p=P)
                sp.dma_start(m_raw[:, m % 2, :].rearrange("p (k n) -> p k n", n=CW),
                             src[:, :, bass.ds(i * (2 * CW) + (m % 24) * CW, CW)]).then_inc(m_full[m % 2], 16)

            def load_w(g, src, nk, step=0):
                if g >= 2:
                    sp.wait_ge(w_lo_pool, step + (g - 1))
                    sp.wait_ge(w_lo_dve, step + (g - 1))
                sp.dma_start(w_raw[:, g % 2, 0:nk * CW].rearrange("p (k n) -> p k n", n=CW), src)\
                    .then_inc(w_full[g % 2], 16)

            def load_small(l):
                for dst, src in ((t_w1[0:33, :], hy_w1[l]), (t_w2[0:64, :], hy_w2[l]), (t_w3[0:64, :], hy_w3[l]),
                                 (hyc[0:64, 0:1], hy_b1[l].rearrange("(p o) -> p o", o=1)),
                                 (hyc[0:64, 1:2], hy_freq[l].rearrange("(p o) -> p o", o=1)),
                                 (hyc[0:64, 2:3], hy_b2[l].rearrange("(p o) -> p o", o=1)),
                                 (t_hyb[0:1, :], hy_bias[l].rearrange("(o n) -> o n", o=1)),
                                 (t_feats[0:33, :], k_feats), (t_decay[:], k_decay)):
                    sp.dma_start(dst, src).then_inc(hyw_full, 16)
                sp.dma_start(wdt[:], w_in[l].rearrange("(k p) n -> p k n", p=P)[:, :, OFF_DT:OFF_DT + 16])\
                    .then_inc(wdt_full, 16)

            def load_in(l, j):
                load_w(PLAN[l, "in"][0] + j, w_in[l].rearrange("(k p) n -> p k n", p=P)[:, :, W_IN[j][1]:W_IN[j][1] + CW], 8)

            for l in range(DEPTH):
                if l == 1:
                    load_in(1, 0)
                    load_in(1, 1)
                    for e in ("pe", "act", "dve"):
                        sp.wait_ge(reached[e], 8)
                load_small(l)
                if l == 0:
                    load_in(0, 0)
                    load_in(0, 1)
                    for m in range(MODS_BEFORE + 1):
                        load_mod(m)
                for j in range(2, len(W_IN)):
                    load_in(l, j)
                    if l == 0:
                        load_mod(MODS_BEFORE + j - 1)
                g = PLAN[l, "out"][0]
                src = w_out[l].rearrange("(k p) n -> p k n", p=P)
                if l == 0:
                    load_mod(MODS_BEFORE + MODS_IN - 1)
                m = MODS_BEFORE + MODS_IN
                for j in range(8):
                    load_w(g + j, src[:, 6 * (j % 2):6 * (j % 2) + 6, (j // 2) * CW:(j // 2 + 1) * CW], 6)
                for part, (c0, n) in enumerate(FFN):
                    g = PLAN[l, f"gu{part}"][0]
                    src = w_gu[l].rearrange("(k p) n -> p k n", p=P)
                    with sp.Fori(0, n) as i:
                        for j in range(2):
                            load_w(g + j, src[:, :, bass.ds(i * CW + (c0 * CW + j * DFF), CW)], 8, i * 2)
                            if l == 0:
                                load_mod(m + j, i)
                    m += 2 * n
                    g = PLAN[l, f"down{part}"][0]
                    src = w_down[l].rearrange("(k p) n -> p k n", p=P)
                    with sp.Fori(0, 2) as i:
                        for j in range(4):
                            k0 = 2 * c0 + n * (j % 2)
                            load_w(g + j, src[:, k0:k0 + n, bass.ds(i * (2 * CW) + (j // 2) * CW, CW)], n, i * 4)
            sp.wait_ge(S["y_nat_ready"], 1)
            sp.dma_start(out[0].rearrange("(t p) d -> p t d", p=P), y_nat[:]).then_inc(out_stored, 16)
            sp.wait_ge(out_stored, 16)

        @block.gpsimd
        def _(pool):
            def split(g, step=0):
                pool.wait_ge(w_hi_done, step * 2 + (2 * g + 1))
                nc.gpsimd.tensor_tensor(w_lo[:, g % 2, 0:HALF], w_raw[:, g % 2, 0:HALF],
                                        w_hi[:, g % 2, 0:HALF].bitcast(F32), ALU.subtract).then_inc(w_lo_pool, 1)

            for l in range(DEPTH):
                pool.wait_ge(wdt_full, 16 * (l + 1))
                nc.gpsimd.tensor_copy(wdt_hi[:], wdt[:]).then_inc(wdt_hi_done, 1)
                pool.wait_ge(wdt_hi_done, l + 1)
                nc.gpsimd.tensor_tensor(wdt_lo[:], wdt[:], wdt_hi[:].bitcast(F32), ALU.subtract).then_inc(wdt_split, 1)
                g = PLAN[l, "in"][0]
                for j in range(len(W_IN)):
                    split(g + j)
                for stage, loops, body in (("out", 2, 4), ("gu0", 6, 2), ("down0", 2, 4), ("gu1", 5, 2), ("down1", 2, 4)):
                    g = PLAN[l, stage][0]
                    with pool.Fori(0, loops) as i:
                        for j in range(body):
                            split(g + j, i * body)

        @block.tensor
        def _(pe):
            mm, transpose = nc.tensor.matmul, nc.tensor.transpose
            p = Program(pe, "pe")
            h_at = [0]

            def mod_step(m, step, i=0):
                j, k = step // KD, step % KD
                if step == 0:
                    pe.wait_ge(m_full[m % 2], i * 16 + 16 * (m // 2 + 1))
                last = mm(ps[:, MOD, bass.ds(i * 8 + (4 * m + 2 * j), 2)], m_raw[:, m % 2, k * CW + j * P:k * CW + (j + 1) * P],
                          cact[:, k, :], start=(k == 0), stop=(k == KD - 1))
                if step == 2 * KD - 1:
                    last.then_inc(mod_done, 1)

            def mods(first, chunks):
                for m in range(first, first + chunks):
                    for step in range(2 * KD):
                        mod_step(m, step)

            def product(g, q, first, final, nk, k0, n, hi, lo, step=0, half=0, token_tiles=None, mod=None):
                pe.wait_ge(w_lo_pool, step + (g + 1))
                pe.wait_ge(w_lo_dve, step + (g + 1))
                if first and q >= 2:
                    pe.wait_ge(pair_free[q % 2], half + q // 2)
                b, s = 2 * (q % 2), g % 2
                if token_tiles is None:
                    for j in range(2):
                        o = ps[:, b + j, 0:n]
                        for k in range(nk):
                            w = slice(k * CW + j * P, k * CW + (j + 1) * P)
                            mm(o, w_hi[:, s, w], hi[:, k0 + k, 0:n], start=first and k == 0, stop=False)
                            mm(o, w_hi[:, s, w], lo[:, k0 + k, 0:n], start=False, stop=False)
                            last = mm(o, w_lo[:, s, w], hi[:, k0 + k, 0:n], start=False, stop=final and k == nk - 1)
                            if mod is not None and (j, k) != (1, KD - 1):
                                mod_step(mod[0], j * KD + k, mod[1])
                else:
                    for t in range(token_tiles):
                        o = ps[:, b + t // 2, (t % 2) * CW:(t % 2 + 1) * CW]
                        tok = slice(t * P, (t + 1) * P)
                        for k in range(nk):
                            w = slice(k * CW, (k + 1) * CW)
                            mm(o, hi[:, k, tok], w_hi[:, s, w], start=(k == 0), stop=False)
                            mm(o, hi[:, k, tok], w_lo[:, s, w], start=False, stop=False)
                            last = mm(o, lo[:, k, tok], w_hi[:, s, w], start=False, stop=(k == nk - 1))
                            if mod is not None and t * KD + k < 2 * KD - 1:
                                mod_step(mod[0], t * KD + k, mod[1])
                last.then_inc(w_used, 1)
                if mod is not None:
                    mod_step(mod[0], 2 * KD - 1, mod[1])

            def project(l, stage, nk, n):
                g0, q0 = PLAN[l, stage]
                with pe.Fori(0, 2) as i:
                    for j in range(4):
                        product(g0 + j, q0 + j // 2, j % 2 == 0, j % 2 == 1, nk, nk * (j % 2), n, f_hi, f_lo,
                                step=i * 4, half=i)

            def stats(n):
                for k in range(KD):
                    p.after("squares")
                    p.sig(mm(ps[:, STAT, 0:n], ones, sqr[:, k % 2, 0:n], start=(k == 0), stop=(k == KD - 1)), "square_summed")

            def to_features(nat, tiles):
                for f in range(4):
                    for t in range(tiles):
                        last = transpose(ps[:, f, t * P:(t + 1) * P], nat[:, t, f * P:(f + 1) * P], ident)
                    p.sig(last, "feat_psum")

            pe.wait_ge(consts_full, 64)
            pe.wait_ge(x_full, 32)
            for k in range(KD):
                if k >= 4:
                    p.after("xT_ready")
                for t in range(4):
                    last = transpose(ps[:, k % 4, t * P:(t + 1) * P], x_nat[:, t, k * P:(k + 1) * P], ident)
                p.sig(last, "x_transposed")
            pe.wait_ge(small_full, 16 * SMALL_LOADS)
            for l in range(DEPTH):
                transpose(ps[:, 6, l * NV:l * NV + NA], stag[0:NA, l, 0, :], ident[0:NA, 0:NA])
                last = transpose(ps[:, 6, l * NV + NA:(l + 1) * NV], stag[0:NB, l, 1, :], ident[0:NB, 0:NB])
            p.sig(last, "vec_transposed")
            p.after("cact_ready")

            for l in range(DEPTH):
                n = tokens(l)
                tiles = n // P
                p.barrier()
                pe.wait_ge(hyw_full, 16 * 9 * (l + 1))
                p.sig(mm(ps[0:64, 6, 0:L], t_w1[0:33, :], t_feats[0:33, :], start=True, stop=True), "filt_psum")
                if l == 0:
                    mods(0, 2)
                p.after("sine_ready")
                p.sig(mm(ps[0:64, 7, 0:L], t_w2[0:64, :], t_h[0:64, 0, :], start=True, stop=True), "filt_psum")
                if l == 0:
                    mods(2, 2)
                p.after("sine_ready")
                for t in range(2):
                    for j in range(2):
                        last = mm(ps[:, 2 * t + j, :], t_h[0:64, 1, t * P:(t + 1) * P], t_w3[0:64, j * 512:(j + 1) * 512],
                                  start=True, stop=True)
                p.sig(last, "filt_psum")
                if l == 0:
                    mods(4, 4)
                p.after("taps_ready")
                for b, col, src in ((0, 0, t_sum), (1, P, t_sum), (2, 4 * P, t_diff), (3, 3 * P, t_diff), (6, 5 * P, t_sum)):
                    for t in range(2):
                        last = mm(ps[:, b, :], c_fwd[:, t, col:col + P], src[:, t, :], start=(t == 0), stop=(t == 1))
                p.sig(last, "spectra_psum")
                p.barrier()
                stats(T)
                pe.wait_ge(wdt_split, l + 1)
                for t in range(4):
                    for k in range(KD):
                        if t == 0:
                            if l == 0 and k < MODS_BEFORE - 8:
                                mods(8 + k, 1)
                            p.after("h_ready")
                        tok, o = slice(t * P, (t + 1) * P), ps[:, 6, t * 16:(t + 1) * 16]
                        mm(o, h_hi[:, k, tok], wdt_hi[:, k, :], start=(k == 0), stop=False)
                        mm(o, h_hi[:, k, tok], wdt_lo[:, k, :], start=False, stop=False)
                        last = mm(o, h_lo[:, k, tok], wdt_hi[:, k, :], start=False, stop=(k == KD - 1))
                p.sig(last, "dt_psum")
                g0, q0 = PLAN[l, "in"]
                for j, (kind, col, idx) in enumerate(W_IN):
                    wide = T if kind == "xbc" and idx < 3 else n
                    product(g0 + j, q0 + j, True, True, 8, 0, wide, h_hi, h_lo,
                            token_tiles={"z": tiles, "q": tiles, "kv": 4}.get(kind),
                            mod=(MODS_BEFORE + j, 0) if l == 0 else None)
                p.barrier()
                p.after("adt_ready")
                for t in range(4):
                    mm(ps[:, 6, t * 16:t * 16 + 8], trif, adt[:, t, 0:8], start=True, stop=True)
                    mm(ps[:, 6, t * 16 + 8:t * 16 + 16], trib, adt[:, t, 8:16], start=True, stop=True)
                    last = mm(ps[:, 6, 64 + t * 16:64 + t * 16 + 16], ones, adt[:, t, :], start=True, stop=True)
                p.sig(last, "cums_psum")
                for t in range(4):
                    for k in range(4):
                        transpose(ps[:, t, k * P:(k + 1) * P], xbc[:, k, t * P:(t + 1) * P], ident)
                    for k in range(2):
                        o = (t % 2) * GN + k * P
                        last = transpose(ps[:, 5 + 2 * (t // 2), o:o + P], xbc[:, 4 + k, t * P:(t + 1) * P], ident)
                    p.sig(last, "xs_transposed")
                p.after("xsn_ready", 4)
                for t in range(tiles):
                    for gr in range(2):
                        tok = slice(t * P, (t + 1) * P)
                        mm(ps[:, gr, tok], xbc[:, 4 + gr, tok], xbc[:, 6 + gr, tok], start=True, stop=True)
                p.after("bnat_ready")
                for t in range(tiles):
                    last = transpose(ps[0:16, 5, t * P:(t + 1) * P], cs[:, t, :], ident)
                p.sig(last, "g_cst_psum")
                p.after("g_cst_ready")
                for h in range(HEADS + 1):
                    if h > 0:
                        p.after("diff_ready")
                    if h < HEADS:
                        for d in range(2):
                            i = d * HEADS + h
                            last = mm(ps[:, 6 + d, 0:n], ident[0:16, i:i + 1].to_broadcast([16, P]), csT[0:16, 0:n],
                                      start=True, stop=True)
                        p.sig(last, "cum_rows")
                    if h > 0:
                        p.after("mt_ready")
                        hd = slice((h - 1) * HD, h * HD)
                        for t in range(tiles):
                            for d in range(2):
                                last = mm(ps[:, t, hd], mt[:, 2 * ((h - 1) % 2) + d, t * P:(t + 1) * P], xsn[:, t, hd],
                                          start=(d == 0), stop=(d == 1))
                        p.sig(last, "y_head_done")
                for d in range(2):
                    for s, t in enumerate(tile_orders(d)):
                        if s > 0:
                            p.after("state_ready")
                            if t < tiles:
                                for gr in range(2):
                                    last = mm(ps[:, 6, gr * 256:(gr + 1) * 256], xbc[:, 6 + gr, t * P:(t + 1) * P],
                                              state[:, gr * 256:(gr + 1) * 256], start=True, stop=True)
                                p.sig(last, "yoff_psum")
                        if s < 3:
                            p.after("xw_ready")
                            for gr in range(2):
                                last = mm(ps[:, 5, gr * 256:(gr + 1) * 256], bnat[:, t, gr * P:(gr + 1) * P],
                                          xw[:, gr * 256:(gr + 1) * 256], start=True, stop=True)
                            p.sig(last, "state_psum")
                p.after("y_normed")
                to_features(ysum, tiles)
                p.barrier()
                for t in range(4):
                    p.after("heads_ready")
                    if t < tiles:
                        for b in range(4):
                            transpose(ps[:, t % 2, b * P:(b + 1) * P], qkn[:, b * P:(b + 1) * P], ident)
                    p.sig(transpose(ps[:, 2 + t % 2, 0:P], qkn[:, 512:QKW], ident), "heads_transposed")
                    p.after("qkT_ready")
                units = [(t, u) for t in range(tiles) for u in range(8)]
                for i in range(len(units) + 2):
                    if i < len(units):
                        t, u = units[i]
                        j, b = u % 2, u // 2
                        k0, keys = (0, T) if t < 2 else (L, L)
                        row = slice(64 * j, 64 * j + 64)
                        p.sig(mm(ps[:, i % 2, 0:keys], qT[row, b, t * P:(t + 1) * P], kT[row, k0:k0 + keys],
                                 start=True, stop=True), "scores")
                    if 1 <= i <= len(units):
                        t, u = units[i - 1]
                        p.after("probs_ready")
                        for kk in range(4 if t < 2 else 2):
                            last = transpose(ps[:, 2 + (i - 1) % 2, kk * P:(kk + 1) * P], prob[:, (i - 1) % 2, kk * P:(kk + 1) * P], ident)
                        p.sig(last, "probT_psum")
                    if i >= 2:
                        t, u = units[i - 2]
                        if u == 0 and t >= 2:
                            p.after("o_ready")
                        j, b = u % 2, u // 2
                        p.after("probT_ready")
                        nk, v0 = (4, 0) if t < 2 else (2, 2)
                        o = ps[:, 6 + t % 2, (b + 4 * j) * HD:(b + 4 * j + 1) * HD]
                        for kk in range(nk):
                            last = mm(o, probT[:, i % 2, kk * P:(kk + 1) * P], v_nat[:, v0 + kk, j * HD:(j + 1) * HD],
                                      start=(kk == 0), stop=(kk == nk - 1))
                        p.sig(last, "pv_done")
                p.after("o_ready", min(tiles, 2))
                p.after("o_normed")
                to_features(onat, tiles)
                p.barrier()
                for t in range(tiles):
                    for k in range(4):
                        last = transpose(ps[:, t, k * P:(k + 1) * P], hyv[:, k, t * P:(t + 1) * P], ident)
                    p.sig(last, "vx_transposed")
                p.after("vn_ready", tiles)
                for s in range(n // L):
                    for f in range(NFREQ):
                        for t in range(2):
                            last = mm(ps[:, f, :], c_fwd[:, t, f * P:(f + 1) * P], vn[:, 2 * s + t, :], start=(t == 0), stop=(t == 1))
                    p.sig(last, "spec_psum")
                    p.after("yspec_ready")
                    for cb in range(4):
                        for f in range(NFREQ):
                            last = mm(ps[:, CONV_BANK[cb], 0:L], yspec[:, f, cb * P:(cb + 1) * P], c_inv[:, f, :],
                                      start=(f == 0), stop=(f == NFREQ - 1))
                    p.sig(last, "conv_psum")
                    p.after("yhy_part")
                for k in range(4):
                    p.after("hy_sq")
                    p.sig(mm(ps[:, STAT, 0:n], ones, hsq[:, 0:n], start=(k == 0), stop=(k == 3)), "hy_summed")
                p.barrier()
                project(l, "out", 6, n)
                p.barrier()
                stats(n)
                p.after("h_ready", KD)
                m = MODS_BEFORE + MODS_IN
                for part, (c0, cnt) in enumerate(FFN):
                    g0, q0 = PLAN[l, f"gu{part}"]
                    with pe.Fori(0, cnt) as i:
                        for j in range(2):
                            product(g0 + j, q0 + j, True, True, 8, 0, n, h_hi, h_lo, step=i * 2, half=i,
                                    mod=(m + j, i) if l == 0 else None)
                    m += 2 * cnt
                    pe.wait_ge(ffn_lo, ffn_at(l, part) + cnt)
                    project(l, f"down{part}", cnt, n)
                p.barrier()
            stats(L)
            for k in range(KD):
                p.after("y_fin_ready")
                for t in range(2):
                    last = transpose(ps[:, (k // 4) * 2 + t, (k % 4) * P:(k % 4 + 1) * P], y_fin[:, k, t * P:(t + 1) * P], ident)
                p.sig(last, "y_fin_psum")

        @block.scalar
        def _(act):
            A = nc.scalar.activation
            p = Program(act, "act")
            loads = []
            for l in range(DEPTH):
                for row, v, cnt in ((V_BMOD, b_mod[l], 48), (V_N1, norm1_g[l], 8), (V_N2, norm2_g[l], 8),
                                    (V_SSDG, ssd_norm_g[l], 4), (V_ATTG, attn_norm_g[l], 4), (V_HYG, hy_norm_g[l], 4),
                                    (V_SCB, ssd_conv_b[l], 8), (V_HCB, hy_conv_b[l], 12), (V_FIN, final_g, 8)):
                    loads.append((stag[row:row + cnt, l, 0, :], v.rearrange("(j p) -> j p", p=P)))
                for row, v, cnt in ((V_SCW, ssd_conv_w[l], 24), (V_HCW, hy_conv_w[l], 36)):
                    for w in range(3):
                        loads.append((stag[row - NA + w * cnt // 3:row - NA + (w + 1) * cnt // 3, l, 1, :],
                                      v[w].rearrange("(j p) -> j p", p=P)))
                for row, v in ((V_C, c[0]), (V_CC, c_ctx)):
                    loads.append((stag[row - NA:row - NA + 8, l, 1, :], v.rearrange("(j p) -> j p", p=P)))
                for dst, v, cnt in ((bc16[:, l, 0, 0:8], ssd_dt_bias[l, 0], 8), (bc16[:, l, 0, 8:16], ssd_dt_bias[l, 1], 8),
                                    (bc16[:, l, 1, 0:8], ssd_a_log[l, 0], 8), (bc16[:, l, 1, 8:16], ssd_a_log[l, 1], 8),
                                    (bc16[:, l, 2, 0:8], ssd_d[l], 8), (qkg[:, l, 0, :], q_norm_g[l], HD),
                                    (qkg[:, l, 1, :], k_norm_g[l], HD)):
                    loads.append((dst, v.rearrange("(o h) -> o h", o=1).to_broadcast([P, cnt])))
            assert len(loads) == SMALL_LOADS, len(loads)
            for dst, src in loads:
                act.dma_start(dst, src).then_inc(small_full, 16)

            def norm(n, src):
                for k in range(KD):
                    if k >= 2:
                        p.after("square_summed")
                    p.sig(A(sqr[:, k % 2, 0:n], src[:, k, 0:n], ACT.Square), "squares")
                p.after("square_summed", 2)
                p.chain(A(lnt[:, 0:n], ps[:, STAT, 0:n], ACT.Ln, scale=1.0 / D, bias=eps1[:, 0:1]))
                p.sig(A(rstd[:, 0:n], lnt[:, 0:n], ACT.Exp, scale=-0.5), "rstd_ready")

            def round_h(n):
                for k in range(KD):
                    p.after("hm_ready")
                    p.sig(A(h_hi[:, k, 0:n], hm[:, k % 2, 0:n], ACT.Copy), "h_hi_ready")

            def round_features(l, blk0, gcol, n):
                for f in range(4):
                    p.after("feat_psum")
                    p.sig(A(f_hi[:, blk0 + f, 0:n], ps[:, f, 0:n], ACT.Identity, scale=vecT[:, l, gcol + f:gcol + f + 1]), "f_hi_ready")

            def token_rms(nat, scratch, tiles, name):
                for t in range(tiles):
                    p.chain(A(scratch, nat[:, t, :], ACT.Square, accum_out=st4[:, t:t + 1]))
                p.chain(A(st4[:, 0:tiles], st4[:, 0:tiles], ACT.Ln, scale=1.0 / 512, bias=eps1[:, 0:1]))
                p.sig(A(st4[:, 0:tiles], st4[:, 0:tiles], ACT.Exp, scale=-0.5), name)

            def round_w(g, step=0, half=0):
                act.wait_ge(w_full[g % 2], half * 16 + 16 * (g // 2 + 1))
                if g >= 2:
                    act.wait_ge(w_used, step + (g - 1))
                for a in (0, HALF):
                    A(w_hi[:, g % 2, a:a + HALF], w_raw[:, g % 2, a:a + HALF], ACT.Copy).then_inc(w_hi_done, 1)

            for k in range(KD):
                p.after("x_transposed")
                p.sig(A(xT[:, k, :], ps[:, k % 4, :], ACT.Copy), "xT_ready")
            p.after("vec_transposed")
            p.link(A(vecT[:].rearrange("p l v -> p (l v)"), ps[:, 6, 0:DEPTH * NV], ACT.Copy))
            act.wait_ge(small_full, 16 * SMALL_LOADS)
            for l in range(DEPTH):
                p.link(A(bc16[:, l, 1, :], bc16[:, l, 1, :], ACT.Exp))
            p.settle()
            A(cact[:, :, 0], vecT[:, 0, V_C:V_C + 8], ACT.Silu)
            p.sig(A(cact[:, :, 1], vecT[:, 0, V_CC:V_CC + 8], ACT.Silu), "cact_ready")

            for l in range(DEPTH):
                n = tokens(l)
                tiles = n // P
                p.barrier()
                for i in range(2):
                    p.after("arg_ready")
                    p.sig(A(t_h[0:64, i, :], t_arg[0:64, :], ACT.Sin), "sine_ready")
                p.barrier()
                if l == 0:
                    round_w(0)
                    round_w(1)
                norm(T, xT)
                round_h(T)
                g0, q0 = PLAN[l, "in"]
                waiting = None
                for j, (kind, col, idx) in enumerate(W_IN):
                    g, q = g0 + j, q0 + j
                    b = 2 * (q % 2)
                    round_w(g + 2)
                    if kind in ("xbc", "hy"):
                        act.wait_ge(w_used, g + 1)
                        for jj in range(2):
                            blk = 2 * idx + jj
                            if kind == "xbc":
                                wide = T if idx < 3 else n
                                dst, wc, bc = xbc[:, blk, 0:wide], V_SCW + 8 + blk, V_SCB + blk
                            else:
                                wide = n
                                dst = (hyv, x1, x0)[blk // 4][:, blk % 4, 0:n]
                                wc, bc = V_HCW + 12 + blk, V_HCB + blk
                            A(dst, ps[:, b + jj, 0:wide], ACT.Identity, scale=vecT[:, l, wc:wc + 1],
                              bias=vecT[:, l, bc:bc + 1]).then_inc(conv_init, 1)
                    if waiting is not None:
                        wq, wi, ww = waiting
                        act.wait_ge(pair_free[wq % 2], wq // 2 + 1)
                        p.link(A(xbc[:, 2 * wi:2 * wi + 2, 0:ww], xbc[:, 2 * wi:2 * wi + 2, 0:ww], ACT.Silu))
                    waiting = (q, idx, T if idx < 3 else n) if kind == "xbc" else None
                    if kind == "z":
                        act.wait_ge(w_used, g + 1)
                        for bb in range(tiles // 2):
                            last = A(zs[:, 2 * bb:2 * bb + 2, idx * CW:(idx + 1) * CW],
                                     ps[:, b + bb, :].rearrange("p (t n) -> p t n", t=2), ACT.Silu)
                        last.then_inc(pair_free[q % 2], 1)
                p.barrier()
                p.after("dt_abs")
                p.chain(A(dmx[:], dab[:], ACT.Exp, scale=-1.0))
                p.sig(A(dt[:], dmx[:], ACT.Ln, bias=1.0), "softplus_tail")
                for t in range(4):
                    p.after("xs_transposed")
                    p.sig(A(xsn[:, t, :], ps[:, t, :], ACT.Copy), "xsn_ready")
                p.after("decays_arg")
                A(wst[:], wst[:], ACT.Exp)
                A(ecs[:], cs[:], ACT.Exp)
                A(etot[:], tot[:], ACT.Exp)
                p.after("g_cst_psum")
                A(gT[:, :, 0:tiles, :], ps[:, 0:2, 0:n].rearrange("p g (t s) -> p g t s", s=P), ACT.Copy)
                p.sig(A(csT[0:16, 0:n], ps[0:16, 5, 0:n], ACT.Copy), "g_cst_ready")
                for h in range(HEADS):
                    p.after("diff_ready")
                    p.sig(A(em[:, :, 0:n], em[:, :, 0:n], ACT.Exp), "decay_exp")
                p.after("y_gated")
                token_rms(ysum, em[:, 0, :], tiles, "y_rms")
                round_features(l, 0, V_SSDG, n)
                p.barrier()
                p.after("head_ss")
                p.chain(A(rs40[:], rs40[:], ACT.Ln, scale=1.0 / HD, bias=eps1[:, 0:1]))
                p.sig(A(rs40[:], rs40[:], ACT.Exp, scale=-0.5), "head_rms")
                for t in range(4):
                    p.after("heads_transposed")
                    if t < tiles:
                        A(qT[:, :, t * P:(t + 1) * P], ps[:, t % 2, :].rearrange("p (b n) -> p b n", b=4), ACT.Copy)
                    p.sig(A(kT[:, t * P:(t + 1) * P], ps[:, 2 + t % 2, 0:P], ACT.Copy), "qkT_ready")
                for i in range(8 * tiles):
                    t, u = i // 8, i % 8
                    keys = T if t < 2 else L
                    c8 = (t % 2) * 8 + u
                    p.after("row_max")
                    if i >= 2:
                        p.after("probT_psum")
                    if u == 0 and t >= 2:
                        p.after("o_ready")
                    p.sig(A(prob[:, i % 2, 0:keys], ps[:, i % 2, 0:keys], ACT.Exp, bias=sm[:, 0, c8:c8 + 1],
                            accum_out=sm[:, 1, c8:c8 + 1]), "probs_ready")
                p.after("probT_psum", 2)
                p.after("o_ready", min(tiles, 2))
                token_rms(onat, prob[:, 0, :], tiles, "o_rms")
                round_features(l, 4, V_ATTG, n)
                p.barrier()
                for t in range(tiles):
                    p.after("vx_transposed")
                    p.sig(A(vn[:, t, :], ps[:, t, :], ACT.Copy), "vn_ready")
                p.after("yhy_part", n // L)
                for k in range(4):
                    if k:
                        p.after("hy_summed")
                    p.sig(A(hsq[:, 0:n], yhy[:, k, 0:n], ACT.Square), "hy_sq")
                p.after("hy_summed")
                p.chain(A(hsq[:, 0:n], ps[:, STAT, 0:n], ACT.Ln, scale=1.0 / 512, bias=eps1[:, 0:1]))
                p.sig(A(hrs[:, 0:n], hsq[:, 0:n], ACT.Exp, scale=-0.5), "hy_rms")
                for k in range(4):
                    p.after("yhy_normed")
                    p.sig(A(f_hi[:, 8 + k, 0:n], yhy[:, k, 0:n], ACT.Identity, scale=vecT[:, l, V_HYG + k:V_HYG + k + 1]), "f_hi_ready")
                p.barrier()

                def round_stage(stage):
                    g0 = PLAN[l, stage][0]
                    last = l == DEPTH - 1 and stage == "down1"
                    with act.Fori(0, 1 if last else 2) as i:
                        for j in range(4):
                            round_w(g0 + j + 2, i * 4, i * 2)
                    if last:
                        for j in range(4, 6):
                            round_w(g0 + j + 2)

                round_stage("out")
                p.barrier()
                norm(n, xT)
                round_h(n)
                for part, (c0, cnt) in enumerate(FFN):
                    g0, q0 = PLAN[l, f"gu{part}"]
                    bg = 2 * (q0 % 2)
                    with act.Fori(0, cnt) as i:
                        round_w(g0 + 2, i * 2, i)
                        A(gate[:, :, 0:n], ps[:, bg:bg + 2, 0:n], ACT.Silu).then_inc(pair_free[q0 % 2], 1)
                        round_w(g0 + 3, i * 2, i)
                        act.wait_ge(pair_free[(q0 + 1) % 2], i + ((q0 + 1) // 2 + 1))
                        A(f_hi[:, bass.ds(i * 2, 2), 0:n], hidden[:, :, 0:n], ACT.Copy).then_inc(ffn_hi, 1)
                    round_stage(f"down{part}")
                p.barrier()
            norm(L, xT)

        @block.vector
        def _(dve):
            V = nc.vector
            TT, TS, STT = V.tensor_tensor, V.tensor_scalar, V.scalar_tensor_tensor
            p = Program(dve, "dve")

            def modulated(l, which, n):
                p.after("rstd_ready")

                def rest(k):
                    p.after("h_hi_ready")
                    p.sig(TT(h_lo[:, k, 0:n], hm[:, k % 2, 0:n], h_hi[:, k, 0:n].bitcast(F32), ALU.subtract), "h_ready")

                for k in range(KD):
                    if k >= 2:
                        rest(k - 2)
                        p.own("h_ready")
                    p.chain(TT(hf[:, k % 2, 0:n], xT[:, k, 0:n], rstd[:, 0:n], ALU.mult))
                    for s in range(n // L):
                        ins = TS(hm[:, k % 2, s * L:(s + 1) * L], hf[:, k % 2, s * L:(s + 1) * L],
                                 amod[:, l, which, k, s:s + 1], modv[:, l, 24 * which + k, s:s + 1], ALU.mult, ALU.add)
                    p.sig(ins, "hm_ready")
                rest(KD - 2)
                rest(KD - 1)

            def split_w(g, step=0):
                dve.wait_ge(w_hi_done, step * 2 + (2 * g + 2))
                TT(w_lo[:, g % 2, HALF:2 * HALF], w_raw[:, g % 2, HALF:2 * HALF],
                   w_hi[:, g % 2, HALF:2 * HALF].bitcast(F32), ALU.subtract).then_inc(w_lo_dve, 1)

            def split_features(l, blk0, gcol, n):
                for f in range(4):
                    p.after("feat_psum")
                    p.after("f_hi_ready")
                    STT(out=f_lo[:, blk0 + f, 0:n], in0=ps[:, f, 0:n], scalar=vecT[:, l, gcol + f:gcol + f + 1],
                        in1=f_hi[:, blk0 + f, 0:n].bitcast(F32), op0=ALU.mult, op1=ALU.subtract)

            def read_mod(l, b0, b1):
                o = l * 2 * MODB
                src = ps[:, MOD, o:o + 2 * MODB].rearrange("p (b s) -> p b s", s=2)
                for s in range(2):
                    p.link(TT(modv[:, l, b0:b1, s], src[:, b0:b1, s], vecT[:, l, V_BMOD + b0:V_BMOD + b1], ALU.add))
                p.settle()

            def scale_mod(l, which):
                for s in range(2):
                    p.link(STT(out=amod[:, l, which, :, s], in0=modv[:, l, 24 * which + 8:24 * which + 16, s], scalar=1.0,
                               in1=vecT[:, l, V_N1 + 8 * which:V_N1 + 8 * which + 8], op0=ALU.add, op1=ALU.mult))
                p.settle()

            def residual(l, stage, gate_blk, n):
                g0, q0 = PLAN[l, stage]

                def two_pairs(i, splits):
                    for pr in range(2):
                        q = q0 + pr
                        b = 2 * (q % 2)
                        if splits > 2 * pr:
                            split_w(g0 + 2 * pr + 2, i * 4)
                        dve.wait_ge(w_used, i * 4 + (g0 + 2 * pr + 2))
                        for jj in range(2):
                            blk = 2 * pr + jj
                            for s in range(n // L):
                                res = xT[:, bass.ds(i * 4 + blk, 1), s * L:(s + 1) * L].rearrange("p o n -> p (o n)")
                                ins = STT(out=res, in0=ps[:, b + jj, s * L:(s + 1) * L],
                                          scalar=modv[:, l, bass.ds(i * 4 + (blk + gate_blk), 1), s:s + 1].rearrange("p o s -> p (o s)"),
                                          in1=res, op0=ALU.mult, op1=ALU.add)
                        ins.then_inc(pair_free[q % 2], 1)
                        if splits > 2 * pr:
                            split_w(g0 + 2 * pr + 3, i * 4)

                last = g0 + 7 == LAST_CHUNK
                with dve.Fori(0, 1 if last else 2) as i:
                    two_pairs(i, 4)
                if last:
                    two_pairs(1, 2)

            V.memset(eps1[:, 0:1], EPS)
            p.after("cact_ready")
            for l in range(DEPTH):
                p.link(TS(bc16[:, l, 1, :], bc16[:, l, 1, :], -1.0, None, ALU.mult))
                p.link(TS(qkg[:, l, 0, :], qkg[:, l, 0, :], HD ** -0.5, None, ALU.mult))
            p.settle()

            for l in range(DEPTH):
                n = tokens(l)
                tiles = n // P
                p.barrier()
                for i in range(2):
                    p.after("filt_psum")
                    p.chain(TS(t_arg[0:64, :], ps[0:64, 6 + i, 0:L], hyc[0:64, 2 * i:2 * i + 1], hyc[0:64, 1:2], ALU.add, ALU.mult))
                    p.chain(TS(t_k[0:64, :], t_arg[0:64, :], 0.15915494309189535, 12582912.0, ALU.mult, ALU.add))
                    p.chain(TS(t_k[0:64, :], t_k[0:64, :], 12582912.0, None, ALU.subtract))
                    for part in (6.28125, 1.9350051879882812e-03, 3.0199159819567e-07):
                        p.chain(STT(out=t_arg[0:64, :], in0=t_k[0:64, :], scalar=-part, in1=t_arg[0:64, :], op0=ALU.mult, op1=ALU.add))
                    p.sig(TS(t_arg[0:64, :], t_arg[0:64, :], 3.1415925, -3.1415925, ALU.min, ALU.max), "arg_ready")
                p.after("filt_psum")
                for t in range(2):
                    for j in range(2):
                        p.link(TT(t_filt[:, t, j * 512:(j + 1) * 512], ps[:, 2 * t + j, :], t_decay[:, t, :], ALU.mult))
                p.settle()
                p.chain(V.memset(t_filt[0:1, 0, 512:1024], 0.0))
                p.link(TT(t_sum[:], t_filt[:, :, 0:512], t_filt[:, :, 512:1024], ALU.add))
                p.link(TT(t_diff[:], t_filt[:, :, 0:512], t_filt[:, :, 512:1024], ALU.subtract))
                p.settle()
                p.sig(TT(t_sum[0:1, 0, :], t_sum[0:1, 0, :], t_hyb[0:1, :], ALU.add), "taps_ready")
                p.after("spectra_psum")
                V.tensor_copy(spec[:, 0:4, :], ps[:, 0:4, :])
                V.tensor_copy(spec[:, 4, :], ps[:, 6, :])
                if l == 0:
                    dve.wait_ge(mod_done, 8)
                    read_mod(0, 0, 16)
                    scale_mod(0, 0)
                else:
                    dve.wait_ge(mod_done, MODS)
                    read_mod(1, 0, MODB)
                    scale_mod(1, 0)
                    scale_mod(1, 1)
                p.barrier()
                if l == 0:
                    split_w(0)
                    split_w(1)
                modulated(l, 0, T)
                p.after("dt_psum")
                p.link(TT(dtr[:], ps[:, 6, 0:64].rearrange("p (t i) -> p t i", i=16),
                          bc16[:, l, 0:1, :].to_broadcast([P, 4, 16]), ALU.add))
                g0, q0 = PLAN[l, "in"]
                blocks = l * 2 * CONV_CHUNKS
                for j, (kind, col, idx) in enumerate(W_IN):
                    g, q = g0 + j, q0 + j
                    b = 2 * (q % 2)
                    split_w(g + 2)
                    if kind in ("xbc", "hy"):
                        wide = T if kind == "xbc" and idx < 3 else n
                        cols = []
                        for jj in range(2):
                            blk = 2 * idx + jj
                            dst = xbc[:, blk, 0:wide] if kind == "xbc" else (hyv, x1, x0)[blk // 4][:, blk % 4, 0:n]
                            w0, w2 = (V_SCW + blk, V_SCW + 16 + blk) if kind == "xbc" else (V_HCW + blk, V_HCW + 24 + blk)
                            cols.append((dst.rearrange("p (s t) -> p s t", t=L),
                                         ps[:, b + jj, 0:wide].rearrange("p (s t) -> p s t", t=L), w0, w2))
                        for d3, p3, w0, w2 in cols:
                            blocks += 1
                            dve.wait_ge(conv_init, blocks)
                            p.link(STT(out=d3[:, :, 1:L], in0=p3[:, :, 0:L - 1], scalar=vecT[:, l, w0:w0 + 1],
                                       in1=d3[:, :, 1:L], op0=ALU.mult, op1=ALU.add))
                        p.settle()
                        for d3, p3, w0, w2 in cols:
                            ins = STT(out=d3[:, :, 0:L - 1], in0=p3[:, :, 1:L], scalar=vecT[:, l, w2:w2 + 1],
                                      in1=d3[:, :, 0:L - 1], op0=ALU.mult, op1=ALU.add)
                        ins.then_inc(pair_free[q % 2], 1)
                        if kind == "hy" and 2 <= idx < 4:
                            dve.wait_ge(pair_free[q % 2], q // 2 + 1)
                            s = slice(2 * (idx - 2), 2 * (idx - 2) + 2)
                            TT(hyv[:, s, 0:n], hyv[:, s, 0:n], x1[:, s, 0:n], ALU.mult)
                    elif kind in ("kv", "q"):
                        dve.wait_ge(w_used, g + 1)
                        for bb in range(2 if kind == "kv" else tiles // 2):
                            src = ps[:, b + bb, :].rearrange("p (t n) -> p t n", t=2)
                            tt = slice(2 * bb, 2 * bb + 2)
                            if kind == "kv":
                                V.tensor_copy(v_nat[:, tt, :], src[:, :, 128:256])
                                ins = V.tensor_copy(qk[:, tt, 512:QKW], src[:, :, 0:128])
                            else:
                                ins = V.tensor_copy(qk[:, tt, idx * CW:(idx + 1) * CW], src)
                        ins.then_inc(pair_free[q % 2], 1)
                p.barrier()
                p.sig(STT(out=dab[:], in0=dtr[:], scalar=-1.0, in1=dtr[:], op0=ALU.mult, op1=ALU.max), "dt_abs")
                p.chain(TS(dtr[:], dtr[:], 0.0, None, ALU.max))
                p.after("softplus_tail")
                p.chain(TT(dt[:], dt[:], dtr[:], ALU.add))
                p.sig(TT(adt[:], dt[:], bc16[:, l, 1:2, :].to_broadcast([P, 4, 16]), ALU.mult), "adt_ready")
                p.after("cums_psum")
                sums = ps[:, 6, 0:P].rearrange("p (a t i) -> p a t i", a=2, i=16)
                p.link(V.tensor_copy(cs[:], sums[:, 0]))
                p.link(V.tensor_copy(tot[:], sums[:, 1]))
                p.settle()
                p.link(TS(ncs[:], cs[:], -1.0, None, ALU.mult))
                p.sig(TT(wst[:], tot[:], cs[:], ALU.subtract), "decays_arg")
                p.after("xs_transposed", 4)
                V.tensor_copy(bnat[:, 0:2, :], ps[:, 5, :].rearrange("p (t n) -> p t n", t=2))
                p.sig(V.tensor_copy(bnat[:, 2:4, :], ps[:, 7, :].rearrange("p (t n) -> p t n", t=2)), "bnat_ready")
                p.after("g_cst_ready")
                p.link(TT(wst[:], wst[:], dt[:], ALU.mult))
                p.settle()
                for h in range(HEADS + 1):
                    if h > 0:
                        hh = h - 1
                        p.after("decay_exp")
                        if hh >= 2:
                            p.after("y_head_done")
                        for d in range(2):
                            for t in range(tiles):
                                ins = STT(out=mt[:, 2 * (hh % 2) + d, t * P:(t + 1) * P], in0=em[:, d, t * P:(t + 1) * P],
                                          scalar=dt[:, t, d * 8 + hh:d * 8 + hh + 1], in1=gT[:, hh // 4, t, :],
                                          op0=ALU.mult, op1=ALU.mult)
                        p.sig(ins, "mt_ready")
                    if h < HEADS:
                        p.after("cum_rows")
                        if h > 0:
                            p.own("mt_ready")
                        for d in range(2):
                            for t in range(tiles):
                                ins = STT(out=em[:, d, t * P:(t + 1) * P], in0=ps[:, 6 + d, t * P:(t + 1) * P],
                                          scalar=ncs[:, t, d * 8 + h:d * 8 + h + 1], in1=c_sq[:, 4 + d, :],
                                          op0=ALU.add, op1=ALU.add)
                        p.sig(ins, "diff_ready")
                p.after("y_head_done", 2)
                for t in range(tiles):
                    p.chain(TT(heads(ysum[:, t, :]), heads(xsn[:, t, :]),
                               bc16[:, l, 2, 0:8].unsqueeze(2).to_broadcast([P, 8, HD]), ALU.mult))
                    p.link(TT(ysum[:, t, :], ysum[:, t, :], ps[:, t, :], ALU.add))
                p.settle()
                for d in range(2):
                    for s, t in enumerate(tile_orders(d)):
                        if s > 0 and t < tiles:
                            p.after("yoff_psum")
                            p.chain(TT(heads(xw[:]), heads(ps[:, 6, :]), per_head(ecs, t, d), ALU.mult))
                            p.chain(TT(ysum[:, t, :], ysum[:, t, :], xw[:], ALU.add))
                        if s < 3:
                            p.sig(TT(heads(xw[:]), heads(xsn[:, t, :]), per_head(wst, t, d), ALU.mult), "xw_ready")
                            if s > 0:
                                p.own("state_ready")
                                p.chain(TT(heads(state[:]), heads(state[:]), per_head(etot, t, d), ALU.mult))
                            p.after("state_psum")
                            if s == 0:
                                p.sig(V.tensor_copy(state[:], ps[:, 5, :]), "state_ready")
                            else:
                                p.sig(TT(state[:], state[:], ps[:, 5, :], ALU.add), "state_ready")
                for t in range(tiles):
                    ins = TT(ysum[:, t, :], ysum[:, t, :], zs[:, t, :], ALU.mult)
                p.sig(ins, "y_gated")
                p.own("y_gated")
                p.after("y_rms")
                for t in range(tiles):
                    ins = TS(ysum[:, t, :], ysum[:, t, :], st4[:, t:t + 1], None, ALU.mult)
                p.sig(ins, "y_normed")
                split_features(l, 0, V_SSDG, n)
                p.barrier()
                for t in range(4):
                    h0 = 0 if t < tiles else 8
                    p.chain(TT(qkn[:, h0 * HD:QKW], qk[:, t, h0 * HD:QKW], qk[:, t, h0 * HD:QKW], ALU.mult))
                    if h0:
                        V.memset(rs40[:, t, 0:8], 1.0)
                    p.link(V.tensor_reduce(out=rs40[:, t, h0:10], in_=heads(qkn[:, h0 * HD:QKW]), op=ALU.add, axis=AX_X))
                    p.settle()
                p.sig(V.memset(sm[:, 2, 15:16], 0.0), "head_ss")
                p.after("head_rms")
                for t in range(4):
                    h0 = 0 if t < tiles else 8
                    q3, k3 = heads(qk[:, t, h0 * HD:QKW]), heads(qk[:, t, 512:QKW])
                    p.chain(TT(q3, q3, rs40[:, t, h0:10].unsqueeze(2).to_broadcast([P, 10 - h0, HD]), ALU.mult))
                    if t < tiles:
                        q4 = heads(qk[:, t, 0:512])
                        p.link(TT(q4, q4, qkg[:, l, 0:1, :].to_broadcast([P, 8, HD]), ALU.mult))
                    p.chain(TT(k3, k3, qkg[:, l, 1:2, :].to_broadcast([P, 2, HD]), ALU.mult))
                    if t > 0:
                        p.after("heads_transposed")
                    dq = qkn[:, 0:512].rearrange("p (b j d) -> p j b d", j=2, d=HD)
                    sq_ = qk[:, t, 0:512].rearrange("p (j b d) -> p j b d", j=2, d=HD)
                    kn = heads(qkn[:, 512:QKW])
                    if t < 2:
                        cosine, sine = c_rope[:, 0, t:t + 1, :], c_rope[:, 1, t, :].rearrange("p (a w d) -> p a w d", w=2, d=16)
                        for j in range(2):
                            p.link(TT(dq[:, j], sq_[:, j], cosine.to_broadcast([P, 4, HD]), ALU.mult))
                        p.link(TT(kn, k3, cosine.to_broadcast([P, 2, HD]), ALU.mult))
                        src = qk[:, t, :].rearrange("p (h a w d) -> p h a w d", a=2, w=2, d=16)
                        dst = ropt[:].rearrange("p (h a w d) -> p h a w d", a=2, w=2, d=16)
                        for w in range(2):
                            for a in range(2):
                                p.link(TT(dst[:, :, a, w, :], src[:, :, a, 1 - w, :],
                                          sine[:, a:a + 1, w, :].to_broadcast([P, 10, 16]), ALU.mult))
                        p.settle()
                        rq = ropt[:, 0:512].rearrange("p (j b d) -> p j b d", j=2, d=HD)
                        for j in range(2):
                            TT(dq[:, j], dq[:, j], rq[:, j], ALU.add)
                        p.sig(TT(qkn[:, 512:QKW], qkn[:, 512:QKW], ropt[:, 512:QKW], ALU.add), "heads_ready")
                    else:
                        if t < tiles:
                            for j in range(2):
                                V.tensor_copy(dq[:, j], sq_[:, j])
                        p.sig(V.tensor_copy(qkn[:, 512:QKW], qk[:, t, 512:QKW]), "heads_ready")
                p.after("heads_transposed")
                for i in range(8 * tiles + 2):
                    if i < 8 * tiles:
                        t, u = i // 8, i % 8
                        c8 = (t % 2) * 8 + u
                        p.after("scores")
                        p.sig(V.tensor_reduce(out=sm[:, 0, c8:c8 + 1], in_=ps[:, i % 2, 0:T if t < 2 else L], op=ALU.max,
                                              axis=AX_X, negate=True), "row_max")
                    if 1 <= i <= 8 * tiles:
                        keys = T if (i - 1) // 8 < 2 else L
                        p.after("probT_psum")
                        if i >= 3:
                            p.after("pv_done")
                        p.sig(V.tensor_copy(probT[:, (i - 1) % 2, 0:keys], ps[:, 2 + (i - 1) % 2, 0:keys]), "probT_ready")
                    if i >= 9 and (i - 1) % 8 == 0 or i == 8 * tiles + 1:
                        t = (i - 2) // 8 if i == 8 * tiles + 1 else (i - 9) // 8
                        if i == 8 * tiles + 1 or t < tiles - 1:
                            dve.wait_ge(S["pv_done"], PV_BEFORE[l] + 8 * (t + 1))
                            dve.wait_ge(S["probs_ready"], PV_BEFORE[l] + 8 * (t + 1))
                            s8 = slice((t % 2) * 8, (t % 2) * 8 + 8)
                            p.chain(V.reciprocal(sm[:, 2, s8], sm[:, 1, s8]))
                            rec = sm[:, 2, s8].rearrange("p (b j) -> p j b", j=2)
                            o4 = onat[:, t, :].rearrange("p (j b d) -> p j b d", j=2, d=HD)
                            v4 = ps[:, 6 + t % 2, :].rearrange("p (j b d) -> p j b d", j=2, d=HD)
                            for j in range(2):
                                ins = TT(o4[:, j], v4[:, j], rec[:, j, :].unsqueeze(2).to_broadcast([P, 4, HD]), ALU.mult)
                            p.sig(ins, "o_ready")
                p.after("pv_done", 2)
                p.own("o_ready")
                p.after("o_rms")
                for t in range(tiles):
                    ins = TS(onat[:, t, :], onat[:, t, :], st4[:, t:t + 1], None, ALU.mult)
                p.sig(ins, "o_normed")
                split_features(l, 4, V_ATTG, n)
                p.barrier()
                for s in range(n // L):
                    p.after("spec_psum")
                    for f in range(2):
                        kr, kim, kr2 = spec[:, f, :], spec[:, 2 + f, :], spec[:, 4 if f == 0 else 1, :]
                        uc, us = ps[:, f, :], ps[:, 2 + f, :]
                        p.link(TT(prod[:, 0, :], us, kim, ALU.mult))
                        p.link(TT(prod[:, 1, :], us, kr2, ALU.mult))
                        p.link(TT(yspec[:, f, :], uc, kr, ALU.mult))
                        p.link(TT(yspec[:, 2 + f, :], uc, kim, ALU.mult))
                        p.settle()
                        p.link(TT(yspec[:, f, :], yspec[:, f, :], prod[:, 0, :], ALU.subtract))
                        ins = TT(yspec[:, 2 + f, :], yspec[:, 2 + f, :], prod[:, 1, :], ALU.add)
                        if f == 0:
                            p.chain(ins)
                    p.sig(ins, "yspec_ready")
                    p.after("conv_psum")
                    for cb in range(4):
                        ins = TT(yhy[:, cb, s * L:(s + 1) * L], ps[:, CONV_BANK[cb], 0:L], x0[:, cb, s * L:(s + 1) * L], ALU.mult)
                    p.sig(ins, "yhy_part")
                p.own("yhy_part")
                p.after("hy_rms")
                for k in range(4):
                    p.sig(TT(yhy[:, k, 0:n], yhy[:, k, 0:n], hrs[:, 0:n], ALU.mult), "yhy_normed")
                p.own("yhy_normed")
                for k in range(4):
                    p.after("f_hi_ready")
                    STT(out=f_lo[:, 8 + k, 0:n], in0=yhy[:, k, 0:n], scalar=vecT[:, l, V_HYG + k:V_HYG + k + 1],
                        in1=f_hi[:, 8 + k, 0:n].bitcast(F32), op0=ALU.mult, op1=ALU.subtract)
                p.barrier()
                if l == 0:
                    dve.wait_ge(mod_done, MODS_BEFORE + MODS_IN)
                    read_mod(0, 16, MODB)
                    scale_mod(0, 1)
                residual(l, "out", 16, n)
                p.barrier()
                modulated(l, 1, n)
                for part, (c0, cnt) in enumerate(FFN):
                    g0, q0 = PLAN[l, f"gu{part}"]
                    bu = 2 * ((q0 + 1) % 2)
                    f0 = ffn_at(l, part)
                    with dve.Fori(0, cnt) as i:
                        split_w(g0 + 2, i * 2)
                        dve.wait_ge(pair_free[q0 % 2], i + (q0 // 2 + 1))
                        dve.wait_ge(w_used, i * 2 + (g0 + 2))
                        TT(hidden[:, :, 0:n], gate[:, :, 0:n], ps[:, bu:bu + 2, 0:n], ALU.mult).then_inc(pair_free[(q0 + 1) % 2], 1)
                        split_w(g0 + 3, i * 2)
                        dve.wait_ge(pair_free[(q0 + 1) % 2], i + ((q0 + 1) // 2 + 1))
                        dve.wait_ge(ffn_hi, i + (f0 + 1))
                        TT(f_lo[:, bass.ds(i * 2, 2), 0:n], hidden[:, :, 0:n],
                           f_hi[:, bass.ds(i * 2, 2), 0:n].bitcast(F32), ALU.subtract).then_inc(ffn_lo, 1)
                        dve.wait_ge(ffn_lo, i + (f0 + 1))
                    residual(l, f"down{part}", 40, n)
                p.barrier()
            p.after("rstd_ready")
            for k in range(KD):
                p.chain(TT(hf[:, k % 2, 0:L], xT[:, k, 0:L], rstd[:, 0:L], ALU.mult))
                p.sig(TS(y_fin[:, k, :], hf[:, k % 2, 0:L], vecT[:, 0, V_FIN + k:V_FIN + k + 1], None, ALU.mult), "y_fin_ready")
            p.after("y_fin_psum", KD)
            for t in range(2):
                for j in range(2):
                    ins = V.tensor_copy(y_nat[:, t, j * 512:(j + 1) * 512], ps[:, 2 * j + t, :])
            p.sig(ins, "y_nat_ready")


_INS = ["x", "c", "ctx", "c_ctx", "w_mod", "b_mod", "norm1_g", "w_in", "ssd_conv_w", "ssd_conv_b", "ssd_a_log",
        "ssd_dt_bias", "ssd_d", "ssd_norm_g", "q_norm_g", "k_norm_g", "attn_norm_g", "hy_conv_w", "hy_conv_b",
        "hy_w1", "hy_b1", "hy_freq", "hy_w2", "hy_b2", "hy_w3", "hy_bias", "hy_norm_g", "w_out", "norm2_g", "w_gu",
        "w_down", "final_g"]
_CONSTS = ["sq", "fwd", "inv", "feats", "decay", "rope"]


def kernel(**inputs):
    import concourse.bacc as bacc
    from concourse.bass_utils import run_bass_kernel_spmd

    nc = bacc.Bacc("TRN2", target_bir_lowering=False, num_devices=1)
    arrays, args = {}, []
    tables = constants()
    for name, a in [(n, inputs[n]) for n in _INS] + [(f"const_{n}", tables[n].astype(np.float32)) for n in _CONSTS]:
        a = np.ascontiguousarray(a)
        arrays[f"in_{name}_dram"] = a
        args.append(nc.dram_tensor(f"in_{name}_dram", a.shape, mybir.dt.from_np(a.dtype), kind="ExternalInput").ap())
    args.append(nc.dram_tensor("out_0_dram", (1, L, D), F32, kind="ExternalOutput").ap())
    backbone(nc, *args)
    r = run_bass_kernel_spmd(nc, [arrays], core_ids=[0])
    return r.results[0]["out_0_dram"]
```

```python
import numpy as np
import concourse.bass as bass
from concourse import mybir
from contextlib import ExitStack

F32 = mybir.dt.float32
F32R = mybir.dt.float32r
ACT = mybir.ActivationFunctionType
ALU = mybir.AluOpType
AX_X = mybir.AxisListType.X

P = 128
D = 1024
L = 256
T = 2 * L
DEPTH = 2
KD = D // P
EPS = 1e-6
HEADS, HD = 8, 64
QKW = (HEADS + 2) * HD
GN = 256
NFREQ = 4
DFF = 2816
MODB = 6 * KD
CW = 256
OFF_K, OFF_XB, OFF_DT, OFF_C, OFF_Q, OFF_Z, OFF_HY = 0, 256, 1024, 1040, 1296, 1808, 2320

V_BMOD, V_N1, V_N2, V_SSDG, V_ATTG, V_HYG, V_SCB, V_HCB, V_FIN = 0, 48, 56, 64, 68, 72, 76, 84, 96
NA = 104
V_SCW, V_HCW, V_C, V_CC = NA, NA + 24, NA + 60, NA + 68
NB = 76
NV = NA + NB

W_IN = ([("xbc", OFF_XB + CW * i, i) for i in range(3)] + [("xbc", OFF_C, 3)]
        + [("z", OFF_Z + CW * i, i) for i in range(2)] + [("kv", OFF_K, 0)]
        + [("q", OFF_Q + CW * i, i) for i in range(2)]
        + [("hy", OFF_HY + CW * i, i) for i in range(6)])
FFN = [(0, 6), (6, 5)]

STAGES = [("in", 15, 15), ("out", 8, 4), ("gu0", 12, 12), ("down0", 8, 4), ("gu1", 10, 10), ("down1", 8, 4)]


def plan():
    at, g, q = {}, 0, 0
    for l in range(DEPTH):
        for name, chunks, pairs in STAGES:
            at[l, name] = (g, q)
            g, q = g + chunks, q + pairs
    return at


PLAN = plan()
LAST_CHUNK = PLAN[DEPTH - 1, "down1"][0] + 7
HALF = 4 * CW
SMALL_LOADS = 18
CONV_CHUNKS = sum(kind in ("xbc", "hy") for kind, _, _ in W_IN)
CONV_BANK = (5, 6, 7, 0)
MODS = DEPTH * MODB // 2
MODS_BEFORE, MODS_IN, MODS_SSD, MODS_ATT = 9, 11, 8, 8
PV_BEFORE = (0, 8 * T // P)


def ffn_at(l, part):
    return l * sum(n for _, n in FFN) + sum(n for _, n in FFN[:part])


def constants():
    f4 = np.float32
    i = np.arange(P)
    sq = np.zeros((P, 6, P), f4)
    sq[:, 0] = np.eye(P)
    sq[:, 1] = 1.0
    sq[:, 2] = i[:, None] <= i[None, :]
    sq[:, 3] = i[:, None] >= i[None, :]
    sq[:, 4] = np.where(i[:, None] <= i[None, :], 0.0, -1e30)
    sq[:, 5] = np.where(i[:, None] >= i[None, :], 0.0, -1e30)
    t = np.arange(L)[:, None].astype(np.float64)
    k = np.arange(L)[None, :].astype(np.float64)
    cos, sin = np.cos(2 * np.pi * k * t / (2 * L)), np.sin(2 * np.pi * k * t / (2 * L))
    alt = (-1.0) ** t
    fwd = np.concatenate([cos, alt, sin[:, 1:], 0 * alt, sin[:, 1:P], alt, cos[:, 1:P]], axis=1)
    fwd = fwd.reshape(2, P, 6 * P).transpose(1, 0, 2)
    w = np.where(k == 0, 1.0, 2.0)
    inv = np.concatenate([(cos * w).T, alt.T, 2 * sin[:, 1:].T], axis=0) / (2 * L)
    inv = inv.reshape(NFREQ, P, L).transpose(1, 0, 2)
    tl = np.linspace(0.0, 1.0, L, dtype=f4)[:, None]
    wl = (2.0 * np.pi * np.arange(L) / L).astype(f4)[:, None]
    fl = np.linspace(1e-4, 15, 16, dtype=f4)
    arg = (fl * wl).astype(f4).astype(np.float64)
    feats = np.concatenate([tl, np.cos(arg), -np.sin(arg)], axis=-1).T
    deltas = np.linspace(np.log(1e-2) / 1.5, np.log(1e-2) / 0.3, 512, dtype=f4)
    decay = np.exp((-tl * np.abs(deltas)).astype(f4).astype(np.float64)).reshape(2, P, 512).transpose(1, 0, 2)
    freq = (10000.0 ** (-np.arange(0, 32, 2) / 32)).astype(f4)
    row, col = np.repeat(np.arange(L // 64), 64).astype(f4), np.tile(np.arange(64), L // 64).astype(f4)
    ar, ac = (row[:, None] * freq).astype(np.float64), (col[:, None] * freq).astype(np.float64)
    rc = np.concatenate([np.cos(ar), np.cos(ar), np.cos(ac), np.cos(ac)], axis=1)
    rs = np.concatenate([-np.sin(ar), np.sin(ar), -np.sin(ac), np.sin(ac)], axis=1)
    rope = np.stack([rc, rs]).reshape(2, 2, P, 64).transpose(2, 0, 1, 3)
    return {"sq": sq, "fwd": fwd, "inv": inv, "feats": feats, "decay": decay, "rope": rope}


def backbone(nc, x, c, ctx_in, c_ctx, w_mod, b_mod, norm1_g, w_in, ssd_conv_w, ssd_conv_b, ssd_a_log,
             ssd_dt_bias, ssd_d, ssd_norm_g, q_norm_g, k_norm_g, attn_norm_g, hy_conv_w, hy_conv_b,
             hy_w1, hy_b1, hy_freq, hy_w2, hy_b2, hy_w3, hy_bias, hy_norm_g, w_out, norm2_g, w_gu,
             w_down, final_g, k_sq, k_fwd, k_inv, k_feats, k_decay, k_rope, out):
    with ExitStack() as stack:
        base = (nc.sbuf_base + 63) // 64 * 64
        KB = 1024

        def at(name, kb, shape, dt=F32):
            return nc.alloc_sbuf_tensor_at(name, [P] + shape, dt, offset=base + int(kb * KB))

        def sem(name):
            return stack.enter_context(nc.semaphore(name))

        xT = at("xT", 0, [KD, T])
        h_hi, h_lo = at("h_hi", 16, [KD, T], F32R), at("h_lo", 32, [KD, T], F32R)
        f_hi, f_lo = at("f_hi", 48, [12, T], F32R), at("f_lo", 72, [12, T], F32R)
        w_raw = at("w_raw", 96, [2, 8 * CW])
        w_hi, w_lo = at("w_hi", 112, [2, 8 * CW], F32R), at("w_lo", 128, [2, 8 * CW], F32R)
        m_raw = at("m_raw", 144, [2, 8 * CW])
        qk = at("qk", 160, [4, QKW])
        v_nat = at("v_nat", 170, [4, 2 * HD])
        spec = at("spec", 172, [5, 512])
        csT = at("csT", 182, [T])
        gate = at("gate", 160, [2, T])
        hidden = at("hidden", 164, [2, T])
        c_sq = at("c_sq", 184, [6, P])
        c_fwd = at("c_fwd", 187, [2, 6 * P])
        c_inv = at("c_inv", 193, [NFREQ, L])
        c_rope = at("c_rope", 197, [2, 2, HD])
        vecT = at("vecT", 198, [DEPTH, NV])
        modv = at("modv", 199.5, [DEPTH, MODB, 2])
        amod = at("amod", 200.25, [DEPTH, 2, KD, 2])
        qkg = at("qkg", 200.5, [DEPTH, 2, HD])
        wdt = at("wdt", 201.5, [8, 16])
        m_row = at("m_row", 201.5, [CW])
        wdt_hi, wdt_lo = at("wdt_hi", 202, [8, 16], F32R), at("wdt_lo", 202.5, [8, 16], F32R)
        bc16 = at("bc16", 203, [DEPTH, 3, 16])
        cact = at("cact", 203.5, [KD, 2])
        hyc = at("hyc", 203.625, [4])
        (dtr, dab, dmx, dt, adt, cs, ncs, tot, wst, ecs, etot) = (
            at(n, 203.75 + 0.25 * i, [4, 16]) for i, n in enumerate(
                ("dtr", "dab", "dmx", "dt", "adt", "cs", "ncs", "tot", "wst", "ecs", "etot")))
        st4 = at("st4", 206.5, [4])
        sm = at("sm", 206.5625, [3, 16])
        rs40 = at("rs40", 206.8125, [4, 10])
        eps1 = at("eps1", 207, [1])
        t_w3, t_decay, t_hyb = at("t_w3", 168, [D]), at("t_decay", 172, [2, 512]), at("t_hyb", 176, [512])
        t_w1, t_w2, t_feats = at("t_w1", 182, [HD]), at("t_w2", 182.25, [HD]), at("t_feats", 182.5, [L])
        t_arg, t_k, t_h = at("t_arg", 64, [L]), at("t_k", 65, [L]), at("t_h", 66, [2, L])
        t_filt = at("t_filt", 68, [2, D])
        t_mod = at("t_mod", 84, [4, 512])
        t_sum, t_diff = at("t_sum", 76, [2, 512]), at("t_diff", 80, [2, 512])
        sqr, hf = at("sqr", 48, [2, T]), at("hf", 52, [2, T])
        hm, rstd = at("hm", 56, [2, T]), at("rstd", 60, [T])
        lnt = at("lnt", 62, [T])
        x_nat = at("x_nat", 16, [4, D])
        stag = at("stag", 32, [DEPTH, 2, P])
        y_nat = at("y_nat", 16, [2, D])
        y_fin = at("y_fin", 32, [KD, L])
        xbc = at("xbc", 48, [8, T])
        x0 = at("x0", 64, [4, T])
        zs = at("zs", 72, [4, 512])
        x1 = at("x1", 80, [4, T])
        hyv = at("hyv", 88, [4, T])
        gT = at("gT", 80, [2, 4, P])
        bnat = at("bnat", 84, [4, GN])
        xsn = at("xsn", 16, [4, 512])
        ysum = at("ysum", 24, [4, 512])
        mt = at("mt", 32, [4, T])
        em = at("em", 40, [4, T])
        yo = at("yo", 44, [512])
        prob, probT = at("prob", 16, [2, T]), at("probT", 20, [2, T])
        qT, kT = at("qT", 24, [4, T]), at("kT", 32, [T])
        onat = at("onat", 34, [4, 512])
        qkn, ropt = at("qkn", 42, [QKW]), at("ropt", 45, [QKW])
        vn = at("vn", 16, [4, 512])
        yspec = at("yspec", 24, [NFREQ, 512])
        prod = at("prod", 32, [2, 512])
        yhy = at("yhy", 36, [4, T])
        hsq = at("hsq", 44, [T])
        hrs = at("hrs", 46, [T])

        ps = stack.enter_context(nc.psum_tensor("ps", [P, 8, 512], F32))
        MOD, STAT = 4, 5
        ident, ones, trif, trib = (c_sq[:, i, :] for i in range(4))

        w_full = [sem("w_full0"), sem("w_full1")]
        w_hi_done = sem("w_hi_done")
        w_lo_pool, w_lo_dve = sem("w_lo_pool"), sem("w_lo_dve")
        w_used = sem("w_used")
        pair_free = [sem("pair_free0"), sem("pair_free1")]
        m_full = [sem("m_full0"), sem("m_full1")]
        mod_done = sem("mod_done")
        consts_full, x_full, small_full, hyw_full = sem("consts_full"), sem("x_full"), sem("small_full"), sem("hyw_full")
        wdt_full, wdt_hi_done, wdt_split = sem("wdt_full"), sem("wdt_hi_done"), sem("wdt_split")
        out_stored = sem("out_stored")
        conv_init = sem("conv_init")
        ffn_hi, ffn_lo = sem("ffn_hi"), sem("ffn_lo")
        reached = {e: sem(f"{e}_reached") for e in ("pe", "act", "dve")}
        S = {name: sem(name) for name in (
            "x_transposed", "xT_ready", "vec_transposed", "cact_ready",
            "eps_ready", "mod_rows_copied", "first_mods", "row_ready", "row_turned", "filt_psum", "spec_ready", "arg_ready", "sine_ready", "taps_ready", "spectra_psum",
            "squares", "square_summed", "rstd_ready", "hf_ready", "hm_ready", "h_hi_ready", "h_ready", "dt_psum", "dt_rows", "dt_turned",
            "dt_abs", "softplus_tail", "adt_ready", "cums_psum", "decays_arg", "xs_transposed", "xsn_ready",
            "bnat_ready", "g_cst_psum", "g_cst_ready", "cum_rows", "diff_ready", "decay_exp", "mt_ready",
            "y_head_done", "state_ready", "yoff_psum", "xw_ready", "state_psum", "yoff_read", "y_gated", "y_rms", "y_normed",
            "feat_psum", "f_hi_ready",
            "head_ss", "head_rms", "heads_ready", "heads_transposed", "qkT_ready", "scores", "row_max",
            "probs_ready", "probT_psum", "probT_ready", "pv_done", "o_ready", "o_rms", "o_normed",
            "vx_transposed", "vn_ready", "spec_psum", "yspec_ready", "conv_psum", "yhy_part",
            "hy_sq", "hy_summed", "hy_rms", "yhy_normed", "y_fin_ready", "y_fin_psum", "y_nat_ready",
            "dve_link", "act_link")}

        class Program:

            def __init__(self, eng, me):
                self.eng, self.me = eng, me
                self.made, self.seen, self.points = {}, {}, 0

            def sig(self, ins, name):
                self.made[name] = self.made.get(name, 0) + 1
                ins.then_inc(S[name], 1)

            def after(self, name, k=1):
                if k == 0:
                    return
                self.seen[name] = self.seen.get(name, 0) + k
                self.eng.wait_ge(S[name], self.seen[name])

            def own(self, name):
                self.eng.wait_ge(S[name], self.made[name])

            def link(self, ins):
                self.sig(ins, f"{self.me}_link")

            def settle(self):
                self.own(f"{self.me}_link")

            def chain(self, ins):
                self.link(ins)
                self.settle()

            def barrier(self):
                self.points += 1
                self.eng.drain().then_inc(reached[self.me], 1)
                for e in ("pe", "act", "dve"):
                    if e != self.me:
                        self.eng.wait_ge(reached[e], self.points)

        def tokens(l):
            return T if l == 0 else L

        def tile_orders(d):
            return (2, 3, 0, 1) if d == 0 else (3, 2, 1, 0)

        updates = [(d, s, tile_orders(d)[s], tile_orders(d)[s + 1]) for d in range(2) for s in range(3)]

        def per_head(src, t, d):
            return src[:, t, 8 * d:8 * d + 8].unsqueeze(2).to_broadcast([P, 8, HD])

        def heads(ap):
            return ap.rearrange("p (h d) -> p h d", d=HD)

        block = stack.enter_context(nc.Block())

        @block.sync
        def _(sp):
            sp.dma_start(x_nat[:, 0:2, :], x[0].rearrange("(t p) d -> p t d", p=P)).then_inc(x_full, 16)
            sp.dma_start(x_nat[:, 2:4, :], ctx_in[0].rearrange("(t p) d -> p t d", p=P)).then_inc(x_full, 16)
            for dst, src in ((c_sq, k_sq), (c_fwd, k_fwd), (c_inv, k_inv), (c_rope, k_rope)):
                sp.dma_start(dst[:], src).then_inc(consts_full, 16)

            def load_mod(m, i=0):
                if m >= 2:
                    sp.wait_ge(mod_done, i * 2 + (m - 1))
                src = w_mod[m // 24].rearrange("(k p) n -> p k n", p=P)
                sp.dma_start(m_raw[:, m % 2, :].rearrange("p (k n) -> p k n", n=CW),
                             src[:, :, bass.ds(i * (2 * CW) + (m % 24) * CW, CW)]).then_inc(m_full[m % 2], 16)

            def load_w(g, src, nk, step=0):
                if g >= 2:
                    sp.wait_ge(w_lo_pool, step + (g - 1))
                    sp.wait_ge(w_lo_dve, step + (g - 1))
                sp.dma_start(w_raw[:, g % 2, 0:nk * CW].rearrange("p (k n) -> p k n", n=CW), src)\
                    .then_inc(w_full[g % 2], 16)

            def load_small(l):
                for dst, src in ((t_w1[0:33, :], hy_w1[l]), (t_w2[0:64, :], hy_w2[l]), (t_w3[0:64, :], hy_w3[l]),
                                 (hyc[0:64, 0:1], hy_b1[l].rearrange("(p o) -> p o", o=1)),
                                 (hyc[0:64, 1:2], hy_freq[l].rearrange("(p o) -> p o", o=1)),
                                 (hyc[0:64, 2:3], hy_b2[l].rearrange("(p o) -> p o", o=1)),
                                 (t_hyb[0:1, :], hy_bias[l].rearrange("(o n) -> o n", o=1)),
                                 (t_feats[0:33, :], k_feats), (t_decay[:], k_decay)):
                    sp.dma_start(dst, src).then_inc(hyw_full, 16)
                sp.dma_start(wdt[:], w_in[l].rearrange("(k p) n -> p k n", p=P)[:, :, OFF_DT:OFF_DT + 16])\
                    .then_inc(wdt_full, 16)

            def load_in(l, j):
                load_w(PLAN[l, "in"][0] + j, w_in[l].rearrange("(k p) n -> p k n", p=P)[:, :, W_IN[j][1]:W_IN[j][1] + CW], 8)

            for l in range(DEPTH):
                if l == 1:
                    for e in ("pe", "act", "dve"):
                        sp.wait_ge(reached[e], 4)
                load_small(l)
                if l == 1:
                    load_in(1, 0)
                    load_in(1, 1)
                if l == 0:
                    load_in(0, 0)
                    load_in(0, 1)
                    for m in range(MODS_BEFORE + 1):
                        load_mod(m)
                for j in range(2, len(W_IN)):
                    load_in(l, j)
                    if l == 0 and j <= MODS_IN:
                        load_mod(MODS_BEFORE + j - 1)
                g = PLAN[l, "out"][0]
                src = w_out[l].rearrange("(k p) n -> p k n", p=P)
                m = MODS_BEFORE + MODS_IN + MODS_SSD + MODS_ATT
                for j in range(8):
                    load_w(g + j, src[:, 6 * (j % 2):6 * (j % 2) + 6, (j // 2) * CW:(j // 2 + 1) * CW], 6)
                    if l == 0 and j == 1:
                        for mc in range(MODS_BEFORE + MODS_IN, m):
                            load_mod(mc)
                for part, (c0, n) in enumerate(FFN):
                    g = PLAN[l, f"gu{part}"][0]
                    src = w_gu[l].rearrange("(k p) n -> p k n", p=P)
                    with sp.Fori(0, n) as i:
                        for j in range(2):
                            load_w(g + j, src[:, :, bass.ds(i * CW + (c0 * CW + j * DFF), CW)], 8, i * 2)
                            if l == 0 and part == 0:
                                load_mod(m + j, i)
                    m += 2 * n
                    g = PLAN[l, f"down{part}"][0]
                    src = w_down[l].rearrange("(k p) n -> p k n", p=P)
                    with sp.Fori(0, 2) as i:
                        for j in range(4):
                            k0 = 2 * c0 + n * (j % 2)
                            load_w(g + j, src[:, k0:k0 + n, bass.ds(i * (2 * CW) + (j // 2) * CW, CW)], n, i * 4)
            sp.wait_ge(S["y_nat_ready"], 1)
            sp.dma_start(out[0].rearrange("(t p) d -> p t d", p=P), y_nat[:]).then_inc(out_stored, 16)
            sp.wait_ge(out_stored, 16)

        @block.gpsimd
        def _(pool):
            def split(g, step=0):
                pool.wait_ge(w_hi_done, step * 2 + (2 * g + 1))
                nc.gpsimd.tensor_tensor(w_lo[:, g % 2, 0:HALF], w_raw[:, g % 2, 0:HALF],
                                        w_hi[:, g % 2, 0:HALF].bitcast(F32), ALU.subtract).then_inc(w_lo_pool, 1)

            for l in range(DEPTH):
                pool.wait_ge(wdt_full, 16 * (l + 1))
                nc.gpsimd.tensor_copy(wdt_hi[:], wdt[:]).then_inc(wdt_hi_done, 1)
                pool.wait_ge(wdt_hi_done, l + 1)
                nc.gpsimd.tensor_tensor(wdt_lo[:], wdt[:], wdt_hi[:].bitcast(F32), ALU.subtract).then_inc(wdt_split, 1)
                g = PLAN[l, "in"][0]
                for j in range(len(W_IN)):
                    split(g + j)
                for stage, loops, body in (("out", 2, 4), ("gu0", 6, 2), ("down0", 2, 4), ("gu1", 5, 2), ("down1", 2, 4)):
                    g = PLAN[l, stage][0]
                    with pool.Fori(0, loops) as i:
                        for j in range(body):
                            split(g + j, i * body)

        @block.tensor
        def _(pe):
            mm, transpose = nc.tensor.matmul, nc.tensor.transpose
            p = Program(pe, "pe")

            def mod_step(m, step, i=0):
                j, k = step // KD, step % KD
                if step == 0:
                    pe.wait_ge(m_full[m % 2], i * 16 + 16 * (m // 2 + 1))
                last = mm(ps[:, MOD, bass.ds(i * 8 + (4 * m + 2 * j), 2)], m_raw[:, m % 2, k * CW + j * P:k * CW + (j + 1) * P],
                          cact[:, k, :], start=(k == 0), stop=(k == KD - 1))
                if step == 2 * KD - 1:
                    last.then_inc(mod_done, 1)

            def mods(first, chunks):
                for m in range(first, first + chunks):
                    for step in range(2 * KD):
                        mod_step(m, step)

            def row_step(m, k0, count):
                if k0 == 0:
                    pe.wait_ge(m_full[m % 2], 16 * (m // 2 + 1))
                o = ps[0:2, 5, 0:CW]
                for k in range(k0, k0 + count):
                    last = mm(o, cact[:, k, :], m_raw[:, m % 2, k * CW:(k + 1) * CW], start=(k == 0), stop=(k == KD - 1))
                if k0 + count == KD:
                    last.then_inc(mod_done, 1)

            def turn_row(m):
                p.after("row_ready")
                for j in range(2):
                    i = 2 * m + j
                    last = transpose(ps[:, MOD, 2 * i:2 * i + 2], m_row[0:2, j * P:(j + 1) * P], ident[0:2, 0:2])
                p.sig(last, "row_turned")

            def product(g, q, first, final, nk, k0, n, hi, lo, step=0, half=0, token_tiles=None, mod=None):
                pe.wait_ge(w_lo_pool, step + (g + 1))
                pe.wait_ge(w_lo_dve, step + (g + 1))
                if first and q >= 2:
                    pe.wait_ge(pair_free[q % 2], half + q // 2)
                b, s = 2 * (q % 2), g % 2
                if token_tiles is None:
                    for j in range(2):
                        o = ps[:, b + j, 0:n]
                        for k in range(nk):
                            w = slice(k * CW + j * P, k * CW + (j + 1) * P)
                            mm(o, w_hi[:, s, w], hi[:, k0 + k, 0:n], start=first and k == 0, stop=False)
                            mm(o, w_hi[:, s, w], lo[:, k0 + k, 0:n], start=False, stop=False)
                            last = mm(o, w_lo[:, s, w], hi[:, k0 + k, 0:n], start=False, stop=final and k == nk - 1)
                            if mod is not None and (j, k) != (1, KD - 1):
                                mod_step(mod[0], j * KD + k, mod[1])
                else:
                    for t in range(token_tiles):
                        o = ps[:, b + t // 2, (t % 2) * CW:(t % 2 + 1) * CW]
                        tok = slice(t * P, (t + 1) * P)
                        for k in range(nk):
                            w = slice(k * CW, (k + 1) * CW)
                            mm(o, hi[:, k, tok], w_hi[:, s, w], start=(k == 0), stop=False)
                            mm(o, hi[:, k, tok], w_lo[:, s, w], start=False, stop=False)
                            last = mm(o, lo[:, k, tok], w_hi[:, s, w], start=False, stop=(k == nk - 1))
                            if mod is not None and t * KD + k < 2 * KD - 1:
                                mod_step(mod[0], t * KD + k, mod[1])
                last.then_inc(w_used, 1)
                if mod is not None:
                    mod_step(mod[0], 2 * KD - 1, mod[1])

            def project(l, stage, nk, n):
                g0, q0 = PLAN[l, stage]
                with pe.Fori(0, 2) as i:
                    for j in range(4):
                        product(g0 + j, q0 + j // 2, j % 2 == 0, j % 2 == 1, nk, nk * (j % 2), n, f_hi, f_lo,
                                step=i * 4, half=i)

            def stats(n):
                for k in range(KD):
                    p.after("squares")
                    p.sig(mm(ps[:, STAT, 0:n], ones, sqr[:, k % 2, 0:n], start=(k == 0), stop=(k == KD - 1)), "square_summed")

            def to_features(nat, tiles):
                for f in range(4):
                    for t in range(tiles):
                        last = transpose(ps[:, f, t * P:(t + 1) * P], nat[:, t, f * P:(f + 1) * P], ident)
                    p.sig(last, "feat_psum")

            pe.wait_ge(consts_full, 64)
            pe.wait_ge(x_full, 32)
            for k in range(KD):
                if k >= 4:
                    p.after("xT_ready")
                for t in range(4):
                    last = transpose(ps[:, k % 4, t * P:(t + 1) * P], x_nat[:, t, k * P:(k + 1) * P], ident)
                p.sig(last, "x_transposed")

            for l in range(DEPTH):
                n = tokens(l)
                tiles = n // P
                pe.wait_ge(hyw_full, 16 * 9 * (l + 1))
                p.sig(mm(ps[0:64, 6, 0:L], t_w1[0:33, :], t_feats[0:33, :], start=True, stop=True), "filt_psum")
                stats(T)
                p.after("sine_ready")
                p.sig(mm(ps[0:64, 7, 0:L], t_w2[0:64, :], t_h[0:64, 0, :], start=True, stop=True), "filt_psum")
                if l == 0:
                    pe.wait_ge(small_full, 16 * SMALL_LOADS)
                    for i in range(DEPTH):
                        transpose(ps[:, 6, i * NV:i * NV + NA], stag[0:NA, i, 0, :], ident[0:NA, 0:NA])
                        last = transpose(ps[:, 6, i * NV + NA:(i + 1) * NV], stag[0:NB, i, 1, :], ident[0:NB, 0:NB])
                    p.sig(last, "vec_transposed")
                    p.after("cact_ready")
                    for m in range(8):
                        pe.wait_ge(m_full[m % 2], 16 * (m // 2 + 1))
                        for k in range(KD):
                            last = mm(ps[0:2, m // 2, (m % 2) * CW:(m % 2 + 1) * CW], cact[:, k, :],
                                      m_raw[:, m % 2, k * CW:(k + 1) * CW], start=(k == 0), stop=(k == KD - 1))
                        last.then_inc(mod_done, 1)
                    for b in range(4):
                        p.after("mod_rows_copied")
                        for j in range(4):
                            i = 4 * b + j
                            last = transpose(ps[:, MOD, 2 * i:2 * i + 2], t_mod[0:2, b, j * P:(j + 1) * P], ident[0:2, 0:2])
                    p.sig(last, "first_mods")
                p.after("sine_ready")
                for t in range(2):
                    for j in range(2):
                        last = mm(ps[:, 2 * t + j, :], t_h[0:64, 1, t * P:(t + 1) * P], t_w3[0:64, j * 512:(j + 1) * 512],
                                  start=True, stop=True)
                p.sig(last, "filt_psum")
                p.after("taps_ready")
                for b, col, src in ((0, 0, t_sum), (1, P, t_sum), (2, 4 * P, t_diff), (3, 3 * P, t_diff), (6, 5 * P, t_sum)):
                    for t in range(2):
                        last = mm(ps[:, b, :], c_fwd[:, t, col:col + P], src[:, t, :], start=(t == 0), stop=(t == 1))
                p.sig(last, "spectra_psum")
                pe.wait_ge(wdt_split, l + 1)
                p.after("spec_ready")
                for k in range(KD):
                    if l == 0 and k < MODS_BEFORE - 8:
                        mods(8 + k, 1)
                    p.after("h_ready")
                    mm(ps[0:16, 6, :], wdt_hi[:, k, :], h_hi[:, k, :], start=(k == 0), stop=False)
                    mm(ps[0:16, 6, :], wdt_lo[:, k, :], h_hi[:, k, :], start=False, stop=False)
                    last = mm(ps[0:16, 6, :], wdt_hi[:, k, :], h_lo[:, k, :], start=False, stop=(k == KD - 1))
                p.sig(last, "dt_psum")
                g0, q0 = PLAN[l, "in"]
                for j, (kind, col, idx) in enumerate(W_IN):
                    wide = T if kind == "xbc" and idx < 3 else n
                    product(g0 + j, q0 + j, True, True, 8, 0, wide, h_hi, h_lo,
                            token_tiles={"z": tiles, "q": tiles, "kv": 4}.get(kind),
                            mod=(MODS_BEFORE + j, 0) if l == 0 and j < MODS_IN else None)
                    if j == 0:
                        p.after("dt_rows")
                        for t in range(4):
                            last = transpose(ps[:, 7, t * 16:(t + 1) * 16], csT[0:16, t * P:(t + 1) * P], ident[0:16, 0:16])
                        p.sig(last, "dt_turned")
                p.barrier()
                p.after("adt_ready")
                for t in range(4):
                    mm(ps[:, 6, t * 16:t * 16 + 8], trif, adt[:, t, 0:8], start=True, stop=True)
                    mm(ps[:, 6, t * 16 + 8:t * 16 + 16], trib, adt[:, t, 8:16], start=True, stop=True)
                    last = mm(ps[:, 6, 64 + t * 16:64 + t * 16 + 16], ones, adt[:, t, :], start=True, stop=True)
                p.sig(last, "cums_psum")
                for t in range(4):
                    for k in range(4):
                        transpose(ps[:, t, k * P:(k + 1) * P], xbc[:, k, t * P:(t + 1) * P], ident)
                    for k in range(2):
                        o = (t % 2) * GN + k * P
                        last = transpose(ps[:, 5 + 2 * (t // 2), o:o + P], xbc[:, 4 + k, t * P:(t + 1) * P], ident)
                    p.sig(last, "xs_transposed")
                p.after("xsn_ready", 4)
                for t in range(tiles):
                    for gr in range(2):
                        tok = slice(t * P, (t + 1) * P)
                        mm(ps[:, gr, tok], xbc[:, 4 + gr, tok], xbc[:, 6 + gr, tok], start=True, stop=True)
                p.after("bnat_ready")
                for t in range(tiles):
                    last = transpose(ps[0:16, 5, t * P:(t + 1) * P], cs[:, t, :], ident)
                p.sig(last, "g_cst_psum")
                p.after("g_cst_ready")
                for h in range(HEADS + 1):
                    if h > 0:
                        p.after("diff_ready")
                    if h < HEADS:
                        for d in range(2):
                            i = d * HEADS + h
                            last = mm(ps[:, 6 + d, 0:n], ident[0:16, i:i + 1].to_broadcast([16, P]), csT[0:16, 0:n],
                                      start=True, stop=True)
                        p.sig(last, "cum_rows")
                    if h > 0:
                        p.after("mt_ready")
                        hd = slice((h - 1) * HD, h * HD)
                        for t in range(tiles):
                            for d in range(2):
                                last = mm(ps[:, t, hd], mt[:, 2 * ((h - 1) % 2) + d, t * P:(t + 1) * P], xsn[:, t, hd],
                                          start=(d == 0), stop=(d == 1))
                        p.sig(last, "y_head_done")
                    if l == 0:
                        if h > 0:
                            turn_row(MODS_BEFORE + MODS_IN + h - 1)
                        if h < HEADS:
                            row_step(MODS_BEFORE + MODS_IN + h, 0, KD)

                def update_psum(u):
                    t = updates[u][2]
                    p.after("xw_ready")
                    for gr in range(2):
                        last = mm(ps[:, 5 + 2 * (u % 2), gr * 256:(gr + 1) * 256], bnat[:, t, gr * P:(gr + 1) * P],
                                  mt[:, u % 2, gr * 256:(gr + 1) * 256], start=True, stop=True)
                    p.sig(last, "state_psum")

                update_psum(0)
                update_psum(1)
                unread = 0
                for u, (d, s, _, reader) in enumerate(updates):
                    p.after("state_ready")
                    if u + 2 < len(updates):
                        update_psum(u + 2)
                    if reader < tiles:
                        p.after("yoff_read", unread)
                        for gr in range(2):
                            last = mm(ps[:, 6, gr * 256:(gr + 1) * 256], xbc[:, 6 + gr, reader * P:(reader + 1) * P],
                                      mt[:, 2 + u % 2, gr * 256:(gr + 1) * 256], start=True, stop=True)
                        p.sig(last, "yoff_psum")
                        unread = 1
                p.after("yoff_read")
                p.after("y_normed")
                to_features(ysum, tiles)
                p.barrier()
                for t in range(4):
                    p.after("heads_ready")
                    if t < tiles:
                        for b in range(4):
                            transpose(ps[:, t % 2, b * P:(b + 1) * P], qkn[:, b * P:(b + 1) * P], ident)
                    p.sig(transpose(ps[:, 2 + t % 2, 0:P], qkn[:, 512:QKW], ident), "heads_transposed")
                    p.after("qkT_ready")
                units = [(t, u) for t in range(tiles) for u in range(8)]
                for i in range(len(units) + 2):
                    if i < len(units):
                        t, u = units[i]
                        j, b = u % 2, u // 2
                        k0, keys = (0, T) if t < 2 else (L, L)
                        row = slice(64 * j, 64 * j + 64)
                        p.sig(mm(ps[:, i % 2, 0:keys], qT[row, b, t * P:(t + 1) * P], kT[row, k0:k0 + keys],
                                 start=True, stop=True), "scores")
                        if l == 0 and i % 4 < 3:
                            row_step(MODS_BEFORE + MODS_IN + MODS_SSD + i // 4, 3 * (i % 4), min(3, KD - 3 * (i % 4)))
                    if 1 <= i <= len(units):
                        t, u = units[i - 1]
                        p.after("probs_ready")
                        for kk in range(4 if t < 2 else 2):
                            last = transpose(ps[:, 2 + (i - 1) % 2, kk * P:(kk + 1) * P], prob[:, (i - 1) % 2, kk * P:(kk + 1) * P], ident)
                        p.sig(last, "probT_psum")
                    if i >= 2:
                        t, u = units[i - 2]
                        if u == 0 and t >= 2:
                            p.after("o_ready")
                        j, b = u % 2, u // 2
                        p.after("probT_ready")
                        nk, v0 = (4, 0) if t < 2 else (2, 2)
                        o = ps[:, 6 + t % 2, (b + 4 * j) * HD:(b + 4 * j + 1) * HD]
                        for kk in range(nk):
                            last = mm(o, probT[:, i % 2, kk * P:(kk + 1) * P], v_nat[:, v0 + kk, j * HD:(j + 1) * HD],
                                      start=(kk == 0), stop=(kk == nk - 1))
                        p.sig(last, "pv_done")
                    if l == 0 and i < len(units) and i % 4 == 3:
                        turn_row(MODS_BEFORE + MODS_IN + MODS_SSD + i // 4)
                p.after("o_ready", min(tiles, 2))
                p.after("o_normed")
                to_features(onat, tiles)
                p.barrier()
                for t in range(tiles):
                    for k in range(4):
                        last = transpose(ps[:, t, k * P:(k + 1) * P], hyv[:, k, t * P:(t + 1) * P], ident)
                    p.sig(last, "vx_transposed")
                p.after("vn_ready", tiles)
                for s in range(n // L):
                    for f in range(NFREQ):
                        for t in range(2):
                            last = mm(ps[:, f, :], c_fwd[:, t, f * P:(f + 1) * P], vn[:, 2 * s + t, :], start=(t == 0), stop=(t == 1))
                    p.sig(last, "spec_psum")
                    p.after("yspec_ready")
                    for cb in range(4):
                        for f in range(NFREQ):
                            last = mm(ps[:, CONV_BANK[cb], 0:L], yspec[:, f, cb * P:(cb + 1) * P], c_inv[:, f, :],
                                      start=(f == 0), stop=(f == NFREQ - 1))
                    p.sig(last, "conv_psum")
                    p.after("yhy_part")
                for k in range(4):
                    p.after("hy_sq")
                    p.sig(mm(ps[:, STAT, 0:n], ones, hsq[:, 0:n], start=(k == 0), stop=(k == 3)), "hy_summed")
                p.barrier()
                project(l, "out", 6, n)
                p.barrier()
                stats(n)
                p.after("h_ready", KD)
                m = MODS_BEFORE + MODS_IN + MODS_SSD + MODS_ATT
                for part, (c0, cnt) in enumerate(FFN):
                    g0, q0 = PLAN[l, f"gu{part}"]
                    with pe.Fori(0, cnt) as i:
                        for j in range(2):
                            product(g0 + j, q0 + j, True, True, 8, 0, n, h_hi, h_lo, step=i * 2, half=i,
                                    mod=(m + j, i) if l == 0 and part == 0 else None)
                    pe.wait_ge(ffn_lo, ffn_at(l, part) + cnt)
                    project(l, f"down{part}", cnt, n)
                p.barrier()
            stats(L)
            for k in range(KD):
                p.after("y_fin_ready")
                for t in range(2):
                    last = transpose(ps[:, (k // 4) * 2 + t, (k % 4) * P:(k % 4 + 1) * P], y_fin[:, k, t * P:(t + 1) * P], ident)
                p.sig(last, "y_fin_psum")

        @block.scalar
        def _(act):
            A = nc.scalar.activation
            p = Program(act, "act")
            loads = []
            for row, v, cnt in ((V_BMOD, b_mod, 48), (V_N1, norm1_g, 8), (V_N2, norm2_g, 8), (V_SSDG, ssd_norm_g, 4),
                                (V_ATTG, attn_norm_g, 4), (V_HYG, hy_norm_g, 4), (V_SCB, ssd_conv_b, 8),
                                (V_HCB, hy_conv_b, 12)):
                loads.append((stag[row:row + cnt, :, 0, :], v.rearrange("l (j p) -> j l p", p=P)))
            for row, v, cnt in ((V_SCW, ssd_conv_w, 24), (V_HCW, hy_conv_w, 36)):
                loads.append((stag[row - NA:row - NA + cnt, :, 1, :], v.rearrange("l w (j p) -> (w j) l p", p=P)))
            for row, v, half in ((V_FIN, final_g, 0), (V_C - NA, c[0], 1), (V_CC - NA, c_ctx, 1)):
                loads.append((stag[row:row + 8, :, half, :],
                              v.rearrange("(j o p) -> j o p", o=1, p=P).to_broadcast([8, DEPTH, P])))
            for dst, v, cnt in ((bc16[:, :, 0, :], ssd_dt_bias.rearrange("l d h -> l (d h)"), 16),
                                (bc16[:, :, 1, :], ssd_a_log.rearrange("l d h -> l (d h)"), 16),
                                (bc16[:, :, 2, 0:8], ssd_d, 8), (qkg[:, :, 0, :], q_norm_g, HD), (qkg[:, :, 1, :], k_norm_g, HD)):
                loads.append((dst, v.rearrange("(o l) h -> o l h", o=1).to_broadcast([P, DEPTH, cnt])))
            assert len(loads) == SMALL_LOADS, len(loads)
            for dst, src in loads:
                act.dma_start(dst, src).then_inc(small_full, 16)

            def norm(n, src):
                for k in range(KD):
                    if k >= 2:
                        p.after("square_summed")
                    p.sig(A(sqr[:, k % 2, 0:n], src[:, k, 0:n], ACT.Square), "squares")
                p.after("square_summed", 2)
                p.chain(A(lnt[:, 0:n], ps[:, STAT, 0:n], ACT.Ln, scale=1.0 / D, bias=eps1[:, 0:1]))
                p.sig(A(rstd[:, 0:n], lnt[:, 0:n], ACT.Exp, scale=-0.5), "rstd_ready")

            def modulate_h(l, which, n, k0=0, k1=KD):
                for k in range(k0, k1):
                    p.after("hf_ready")
                    if k >= 2:
                        p.after("h_ready")
                    for s in range(n // L):
                        tok = slice(s * L, (s + 1) * L)
                        ins = A(hm[:, k % 2, tok], hf[:, k % 2, tok], ACT.Identity, scale=amod[:, l, which, k, s:s + 1],
                                bias=modv[:, l, 24 * which + k, s:s + 1])
                    p.sig(ins, "hm_ready")
                    p.own("hm_ready")
                    p.sig(A(h_hi[:, k, 0:n], hm[:, k % 2, 0:n], ACT.Copy), "h_hi_ready")
                if k1 == KD:
                    p.after("h_ready", 2)

            def sine(i):
                p.after("arg_ready")
                p.sig(A(t_h[0:64, i, :], t_arg[0:64, :], ACT.Sin), "sine_ready")

            def round_features(l, blk0, gcol, n):
                for f in range(4):
                    p.after("feat_psum")
                    p.sig(A(f_hi[:, blk0 + f, 0:n], ps[:, f, 0:n], ACT.Identity, scale=vecT[:, l, gcol + f:gcol + f + 1]), "f_hi_ready")

            def token_rms(nat, scratch, tiles, name):
                for t in range(tiles):
                    p.chain(A(scratch, nat[:, t, :], ACT.Square, accum_out=st4[:, t:t + 1]))
                p.chain(A(st4[:, 0:tiles], st4[:, 0:tiles], ACT.Ln, scale=1.0 / 512, bias=eps1[:, 0:1]))
                p.sig(A(st4[:, 0:tiles], st4[:, 0:tiles], ACT.Exp, scale=-0.5), name)

            def copy_row(m):
                act.wait_ge(mod_done, m + 1)
                if m > MODS_BEFORE + MODS_IN:
                    p.after("row_turned")
                p.sig(A(m_row[0:2, :], ps[0:2, 5, 0:CW], ACT.Copy), "row_ready")

            def round_w(g, step=0, half=0):
                act.wait_ge(w_full[g % 2], half * 16 + 16 * (g // 2 + 1))
                if g >= 2:
                    act.wait_ge(w_used, step + (g - 1))
                for a in (0, HALF):
                    A(w_hi[:, g % 2, a:a + HALF], w_raw[:, g % 2, a:a + HALF], ACT.Copy).then_inc(w_hi_done, 1)

            p.after("eps_ready")
            for k in range(KD):
                p.after("x_transposed")
                p.sig(A(xT[:, k, :], ps[:, k % 4, :], ACT.Copy), "xT_ready")
            for l in range(DEPTH):
                n = tokens(l)
                tiles = n // P
                norm(T, xT)
                sine(0)
                if l == 0:
                    p.after("vec_transposed")
                    p.link(A(vecT[:].rearrange("p l v -> p (l v)"), ps[:, 6, 0:DEPTH * NV], ACT.Copy))
                    act.wait_ge(small_full, 16 * SMALL_LOADS)
                    p.link(A(bc16[:, :, 1, :], bc16[:, :, 1, :], ACT.Exp))
                    p.settle()
                    A(cact[:, :, 0], vecT[:, 0, V_C:V_C + 8], ACT.Silu)
                    p.sig(A(cact[:, :, 1], vecT[:, 0, V_CC:V_CC + 8], ACT.Silu), "cact_ready")
                    sine(1)
                    round_w(0)
                    for b in range(4):
                        act.wait_ge(mod_done, 2 * b + 2)
                        p.sig(A(t_mod[0:2, b, :], ps[0:2, b, :], ACT.Copy), "mod_rows_copied")
                    round_w(1)
                    modulate_h(0, 0, T)
                else:
                    modulate_h(1, 0, T, 0, 2)
                    sine(1)
                    modulate_h(1, 0, T, 2)
                g0, q0 = PLAN[l, "in"]
                waiting = None
                for j, (kind, col, idx) in enumerate(W_IN):
                    g, q = g0 + j, q0 + j
                    b = 2 * (q % 2)
                    round_w(g + 2)
                    if kind in ("xbc", "hy"):
                        act.wait_ge(w_used, g + 1)
                        for jj in range(2):
                            blk = 2 * idx + jj
                            if kind == "xbc":
                                wide = T if idx < 3 else n
                                dst, wc, bc = xbc[:, blk, 0:wide], V_SCW + 8 + blk, V_SCB + blk
                            else:
                                wide = n
                                dst = (hyv, x1, x0)[blk // 4][:, blk % 4, 0:n]
                                wc, bc = V_HCW + 12 + blk, V_HCB + blk
                            A(dst, ps[:, b + jj, 0:wide], ACT.Identity, scale=vecT[:, l, wc:wc + 1],
                              bias=vecT[:, l, bc:bc + 1]).then_inc(conv_init, 1)
                    if waiting is not None:
                        wq, wi, ww = waiting
                        act.wait_ge(pair_free[wq % 2], wq // 2 + 1)
                        p.link(A(xbc[:, 2 * wi:2 * wi + 2, 0:ww], xbc[:, 2 * wi:2 * wi + 2, 0:ww], ACT.Silu))
                    waiting = (q, idx, T if idx < 3 else n) if kind == "xbc" else None
                    if kind == "z":
                        act.wait_ge(w_used, g + 1)
                        for bb in range(tiles // 2):
                            last = A(zs[:, 2 * bb:2 * bb + 2, idx * CW:(idx + 1) * CW],
                                     ps[:, b + bb, :].rearrange("p (t n) -> p t n", t=2), ACT.Silu)
                        last.then_inc(pair_free[q % 2], 1)
                p.barrier()
                p.after("dt_abs")
                p.chain(A(dmx[:], dab[:], ACT.Exp, scale=-1.0))
                p.sig(A(dt[:], dmx[:], ACT.Ln, bias=1.0), "softplus_tail")
                for t in range(4):
                    p.after("xs_transposed")
                    p.sig(A(xsn[:, t, :], ps[:, t, :], ACT.Copy), "xsn_ready")
                p.after("decays_arg")
                A(wst[:], wst[:], ACT.Exp)
                A(ecs[:], cs[:], ACT.Exp)
                A(etot[:], tot[:], ACT.Exp)
                p.after("g_cst_psum")
                A(gT[:, :, 0:tiles, :], ps[:, 0:2, 0:n].rearrange("p g (t s) -> p g t s", s=P), ACT.Copy)
                p.sig(A(csT[0:16, 0:n], ps[0:16, 5, 0:n], ACT.Copy), "g_cst_ready")
                for h in range(HEADS):
                    p.after("diff_ready")
                    e = slice(2 * (h % 2), 2 * (h % 2) + 2)
                    p.sig(A(em[:, e, 0:n], em[:, e, 0:n], ACT.Exp), "decay_exp")
                    if l == 0:
                        copy_row(MODS_BEFORE + MODS_IN + h)
                p.after("y_gated")
                token_rms(ysum, em[:, 0, :], tiles, "y_rms")
                round_features(l, 0, V_SSDG, n)
                p.barrier()
                p.after("head_ss")
                p.chain(A(rs40[:], rs40[:], ACT.Ln, scale=1.0 / HD, bias=eps1[:, 0:1]))
                p.sig(A(rs40[:], rs40[:], ACT.Exp, scale=-0.5), "head_rms")
                for t in range(4):
                    p.after("heads_transposed")
                    if t < tiles:
                        A(qT[:, :, t * P:(t + 1) * P], ps[:, t % 2, :].rearrange("p (b n) -> p b n", b=4), ACT.Copy)
                    p.sig(A(kT[:, t * P:(t + 1) * P], ps[:, 2 + t % 2, 0:P], ACT.Copy), "qkT_ready")
                for i in range(8 * tiles):
                    t, u = i // 8, i % 8
                    keys = T if t < 2 else L
                    c8 = (t % 2) * 8 + u
                    p.after("row_max")
                    if i >= 2:
                        p.after("probT_psum")
                    if u == 0 and t >= 2:
                        p.after("o_ready")
                    p.sig(A(prob[:, i % 2, 0:keys], ps[:, i % 2, 0:keys], ACT.Exp, bias=sm[:, 0, c8:c8 + 1],
                            accum_out=sm[:, 1, c8:c8 + 1]), "probs_ready")
                    if l == 0 and i % 4 == 2:
                        copy_row(MODS_BEFORE + MODS_IN + MODS_SSD + i // 4)
                p.after("probT_psum", 2)
                p.after("o_ready", min(tiles, 2))
                token_rms(onat, prob[:, 0, :], tiles, "o_rms")
                round_features(l, 4, V_ATTG, n)
                p.barrier()
                for t in range(tiles):
                    p.after("vx_transposed")
                    p.sig(A(vn[:, t, :], ps[:, t, :], ACT.Copy), "vn_ready")
                p.after("yhy_part", n // L)
                for k in range(4):
                    if k:
                        p.after("hy_summed")
                    p.sig(A(hsq[:, 0:n], yhy[:, k, 0:n], ACT.Square), "hy_sq")
                p.after("hy_summed")
                p.chain(A(hsq[:, 0:n], ps[:, STAT, 0:n], ACT.Ln, scale=1.0 / 512, bias=eps1[:, 0:1]))
                p.sig(A(hrs[:, 0:n], hsq[:, 0:n], ACT.Exp, scale=-0.5), "hy_rms")
                for k in range(4):
                    p.after("yhy_normed")
                    p.sig(A(f_hi[:, 8 + k, 0:n], yhy[:, k, 0:n], ACT.Identity, scale=vecT[:, l, V_HYG + k:V_HYG + k + 1]), "f_hi_ready")
                p.barrier()

                def round_stage(stage):
                    g0 = PLAN[l, stage][0]
                    last = l == DEPTH - 1 and stage == "down1"
                    with act.Fori(0, 1 if last else 2) as i:
                        for j in range(4):
                            round_w(g0 + j + 2, i * 4, i * 2)
                    if last:
                        for j in range(4, 6):
                            round_w(g0 + j + 2)

                round_stage("out")
                p.barrier()
                norm(n, xT)
                modulate_h(l, 1, n)
                for part, (c0, cnt) in enumerate(FFN):
                    g0, q0 = PLAN[l, f"gu{part}"]
                    bg = 2 * (q0 % 2)
                    with act.Fori(0, cnt) as i:
                        round_w(g0 + 2, i * 2, i)
                        A(gate[:, :, 0:n], ps[:, bg:bg + 2, 0:n], ACT.Silu).then_inc(pair_free[q0 % 2], 1)
                        round_w(g0 + 3, i * 2, i)
                        act.wait_ge(pair_free[(q0 + 1) % 2], i + ((q0 + 1) // 2 + 1))
                        A(f_hi[:, bass.ds(i * 2, 2), 0:n], hidden[:, :, 0:n], ACT.Copy).then_inc(ffn_hi, 1)
                    round_stage(f"down{part}")
                p.barrier()
            norm(L, xT)

        @block.vector
        def _(dve):
            V = nc.vector
            TT, TS, STT = V.tensor_tensor, V.tensor_scalar, V.scalar_tensor_tensor
            p = Program(dve, "dve")

            def normed(n, k0=0, k1=KD):
                if k0 == 0:
                    p.after("rstd_ready")

                def rest(k):
                    p.after("h_hi_ready")
                    p.sig(TT(h_lo[:, k, 0:n], hm[:, k % 2, 0:n], h_hi[:, k, 0:n].bitcast(F32), ALU.subtract), "h_ready")

                for k in range(k0, k1):
                    if k >= 2:
                        rest(k - 2)
                    p.sig(TT(hf[:, k % 2, 0:n], xT[:, k, 0:n], rstd[:, 0:n], ALU.mult), "hf_ready")
                if k1 == KD:
                    rest(KD - 2)
                    rest(KD - 1)

            def split_w(g, step=0):
                dve.wait_ge(w_hi_done, step * 2 + (2 * g + 2))
                TT(w_lo[:, g % 2, HALF:2 * HALF], w_raw[:, g % 2, HALF:2 * HALF],
                   w_hi[:, g % 2, HALF:2 * HALF].bitcast(F32), ALU.subtract).then_inc(w_lo_dve, 1)

            def split_features(l, blk0, gcol, n):
                for f in range(4):
                    p.after("feat_psum")
                    p.after("f_hi_ready")
                    STT(out=f_lo[:, blk0 + f, 0:n], in0=ps[:, f, 0:n], scalar=vecT[:, l, gcol + f:gcol + f + 1],
                        in1=f_hi[:, blk0 + f, 0:n].bitcast(F32), op0=ALU.mult, op1=ALU.subtract)

            def read_mod(l, b0, b1):
                o = l * 2 * MODB
                src = ps[:, MOD, o:o + 2 * MODB].rearrange("p (b s) -> p b s", s=2)
                for s in range(2):
                    p.link(TT(modv[:, l, b0:b1, s], src[:, b0:b1, s], vecT[:, l, V_BMOD + b0:V_BMOD + b1], ALU.add))
                p.settle()

            def scale_mod(l, which):
                for s in range(2):
                    p.link(STT(out=amod[:, l, which, :, s], in0=modv[:, l, 24 * which + 8:24 * which + 16, s], scalar=1.0,
                               in1=vecT[:, l, V_N1 + 8 * which:V_N1 + 8 * which + 8], op0=ALU.add, op1=ALU.mult))
                p.settle()

            def residual(l, stage, gate_blk, n):
                g0, q0 = PLAN[l, stage]

                def two_pairs(i, splits):
                    for pr in range(2):
                        q = q0 + pr
                        b = 2 * (q % 2)
                        if splits > 2 * pr:
                            split_w(g0 + 2 * pr + 2, i * 4)
                        dve.wait_ge(w_used, i * 4 + (g0 + 2 * pr + 2))
                        for jj in range(2):
                            blk = 2 * pr + jj
                            for s in range(n // L):
                                res = xT[:, bass.ds(i * 4 + blk, 1), s * L:(s + 1) * L].rearrange("p o n -> p (o n)")
                                ins = STT(out=res, in0=ps[:, b + jj, s * L:(s + 1) * L],
                                          scalar=modv[:, l, bass.ds(i * 4 + (blk + gate_blk), 1), s:s + 1].rearrange("p o s -> p (o s)"),
                                          in1=res, op0=ALU.mult, op1=ALU.add)
                        ins.then_inc(pair_free[q % 2], 1)
                        if splits > 2 * pr:
                            split_w(g0 + 2 * pr + 3, i * 4)

                last = g0 + 7 == LAST_CHUNK
                with dve.Fori(0, 1 if last else 2) as i:
                    two_pairs(i, 4)
                if last:
                    two_pairs(1, 2)

            p.sig(V.memset(eps1[:, 0:1], EPS), "eps_ready")

            def argument(l, i):
                p.after("filt_psum")
                if i == 1:
                    dve.wait_ge(S["sine_ready"], 2 * l + 1)
                p.chain(TS(t_arg[0:64, :], ps[0:64, 6 + i, 0:L], hyc[0:64, 2 * i:2 * i + 1], hyc[0:64, 1:2], ALU.add, ALU.mult))
                p.chain(TS(t_k[0:64, :], t_arg[0:64, :], 0.15915494309189535, 12582912.0, ALU.mult, ALU.add))
                p.chain(TS(t_k[0:64, :], t_k[0:64, :], 12582912.0, None, ALU.subtract))
                for part in (6.28125, 1.9350051879882812e-03, 3.0199159819567e-07):
                    p.chain(STT(out=t_arg[0:64, :], in0=t_k[0:64, :], scalar=-part, in1=t_arg[0:64, :], op0=ALU.mult, op1=ALU.add))
                p.sig(TS(t_arg[0:64, :], t_arg[0:64, :], 3.1415925, -3.1415925, ALU.min, ALU.max), "arg_ready")

            for l in range(DEPTH):
                n = tokens(l)
                tiles = n // P
                argument(l, 0)
                if l == 0:
                    argument(l, 1)
                    p.after("cact_ready")
                    p.link(TS(bc16[:, :, 1, :], bc16[:, :, 1, :], -1.0, None, ALU.mult))
                    p.link(TS(qkg[:, :, 0, :], qkg[:, :, 0, :], HD ** -0.5, None, ALU.mult))
                    p.settle()
                    p.after("first_mods")
                    read_mod(0, 0, 16)
                    scale_mod(0, 0)
                    split_w(0)
                    split_w(1)
                    normed(T, 0, 2)
                else:
                    dve.wait_ge(mod_done, MODS)
                    read_mod(1, 0, MODB)
                    scale_mod(1, 0)
                    scale_mod(1, 1)
                    normed(T, 0, 2)
                    argument(l, 1)
                p.after("filt_psum")
                for t in range(2):
                    for j in range(2):
                        p.link(TT(t_filt[:, t, j * 512:(j + 1) * 512], ps[:, 2 * t + j, :], t_decay[:, t, :], ALU.mult))
                p.settle()
                p.chain(V.memset(t_filt[0:1, 0, 512:1024], 0.0))
                p.link(TT(t_sum[:], t_filt[:, :, 0:512], t_filt[:, :, 512:1024], ALU.add))
                p.link(TT(t_diff[:], t_filt[:, :, 0:512], t_filt[:, :, 512:1024], ALU.subtract))
                p.settle()
                p.sig(TT(t_sum[0:1, 0, :], t_sum[0:1, 0, :], t_hyb[0:1, :], ALU.add), "taps_ready")
                p.own("taps_ready")
                normed(T, 2, 6)
                p.after("spectra_psum")
                V.tensor_copy(spec[:, 0:4, :], ps[:, 0:4, :])
                p.sig(V.tensor_copy(spec[:, 4, :], ps[:, 6, :]), "spec_ready")
                normed(T, 6)
                p.after("dt_psum")
                p.sig(V.tensor_copy(csT[0:16, :], ps[0:16, 6, :]), "dt_rows")
                p.after("dt_turned")
                p.link(TT(dtr[:], ps[:, 7, 0:64].rearrange("p (t i) -> p t i", i=16),
                          bc16[:, l, 0:1, :].to_broadcast([P, 4, 16]), ALU.add))
                g0, q0 = PLAN[l, "in"]
                blocks = l * 2 * CONV_CHUNKS
                for j, (kind, col, idx) in enumerate(W_IN):
                    g, q = g0 + j, q0 + j
                    b = 2 * (q % 2)
                    split_w(g + 2)
                    if kind in ("xbc", "hy"):
                        wide = T if kind == "xbc" and idx < 3 else n
                        cols = []
                        for jj in range(2):
                            blk = 2 * idx + jj
                            dst = xbc[:, blk, 0:wide] if kind == "xbc" else (hyv, x1, x0)[blk // 4][:, blk % 4, 0:n]
                            w0, w2 = (V_SCW + blk, V_SCW + 16 + blk) if kind == "xbc" else (V_HCW + blk, V_HCW + 24 + blk)
                            cols.append((dst.rearrange("p (s t) -> p s t", t=L),
                                         ps[:, b + jj, 0:wide].rearrange("p (s t) -> p s t", t=L), w0, w2))
                        for d3, p3, w0, w2 in cols:
                            blocks += 1
                            dve.wait_ge(conv_init, blocks)
                            p.link(STT(out=d3[:, :, 1:L], in0=p3[:, :, 0:L - 1], scalar=vecT[:, l, w0:w0 + 1],
                                       in1=d3[:, :, 1:L], op0=ALU.mult, op1=ALU.add))
                        p.settle()
                        for d3, p3, w0, w2 in cols:
                            ins = STT(out=d3[:, :, 0:L - 1], in0=p3[:, :, 1:L], scalar=vecT[:, l, w2:w2 + 1],
                                      in1=d3[:, :, 0:L - 1], op0=ALU.mult, op1=ALU.add)
                        ins.then_inc(pair_free[q % 2], 1)
                        if kind == "hy" and 2 <= idx < 4:
                            dve.wait_ge(pair_free[q % 2], q // 2 + 1)
                            s = slice(2 * (idx - 2), 2 * (idx - 2) + 2)
                            TT(hyv[:, s, 0:n], hyv[:, s, 0:n], x1[:, s, 0:n], ALU.mult)
                    elif kind in ("kv", "q"):
                        dve.wait_ge(w_used, g + 1)
                        for bb in range(2 if kind == "kv" else tiles // 2):
                            src = ps[:, b + bb, :].rearrange("p (t n) -> p t n", t=2)
                            tt = slice(2 * bb, 2 * bb + 2)
                            if kind == "kv":
                                V.tensor_copy(v_nat[:, tt, :], src[:, :, 128:256])
                                ins = V.tensor_copy(qk[:, tt, 512:QKW], src[:, :, 0:128])
                            else:
                                ins = V.tensor_copy(qk[:, tt, idx * CW:(idx + 1) * CW], src)
                        ins.then_inc(pair_free[q % 2], 1)
                p.barrier()
                p.sig(STT(out=dab[:], in0=dtr[:], scalar=-1.0, in1=dtr[:], op0=ALU.mult, op1=ALU.max), "dt_abs")
                p.chain(TS(dtr[:], dtr[:], 0.0, None, ALU.max))
                p.after("softplus_tail")
                p.chain(TT(dt[:], dt[:], dtr[:], ALU.add))
                p.sig(TT(adt[:], dt[:], bc16[:, l, 1:2, :].to_broadcast([P, 4, 16]), ALU.mult), "adt_ready")
                p.after("cums_psum")
                sums = ps[:, 6, 0:P].rearrange("p (a t i) -> p a t i", a=2, i=16)
                p.link(V.tensor_copy(cs[:], sums[:, 0]))
                p.link(V.tensor_copy(tot[:], sums[:, 1]))
                p.settle()
                p.link(TS(ncs[:], cs[:], -1.0, None, ALU.mult))
                p.sig(TT(wst[:], tot[:], cs[:], ALU.subtract), "decays_arg")
                p.after("xs_transposed", 4)
                V.tensor_copy(bnat[:, 0:2, :], ps[:, 5, :].rearrange("p (t n) -> p t n", t=2))
                p.sig(V.tensor_copy(bnat[:, 2:4, :], ps[:, 7, :].rearrange("p (t n) -> p t n", t=2)), "bnat_ready")
                p.after("g_cst_ready")
                p.link(TT(wst[:], wst[:], dt[:], ALU.mult))
                p.settle()
                for h in range(HEADS + 1):
                    if h > 0:
                        hh = h - 1
                        p.after("decay_exp")
                        if hh >= 2:
                            p.after("y_head_done")
                        for d in range(2):
                            for t in range(tiles):
                                ins = STT(out=mt[:, 2 * (hh % 2) + d, t * P:(t + 1) * P],
                                          in0=em[:, 2 * (hh % 2) + d, t * P:(t + 1) * P],
                                          scalar=dt[:, t, d * 8 + hh:d * 8 + hh + 1], in1=gT[:, hh // 4, t, :],
                                          op0=ALU.mult, op1=ALU.mult)
                        p.sig(ins, "mt_ready")
                    if h < HEADS:
                        p.after("cum_rows")
                        if h >= 2:
                            p.own("mt_ready")
                        for d in range(2):
                            for t in range(tiles):
                                ins = STT(out=em[:, 2 * (h % 2) + d, t * P:(t + 1) * P], in0=ps[:, 6 + d, t * P:(t + 1) * P],
                                          scalar=ncs[:, t, d * 8 + h:d * 8 + h + 1], in1=c_sq[:, 4 + d, :],
                                          op0=ALU.add, op1=ALU.add)
                        p.sig(ins, "diff_ready")
                p.after("y_head_done", 2)
                for t in range(tiles):
                    p.chain(TT(heads(ysum[:, t, :]), heads(xsn[:, t, :]),
                               bc16[:, l, 2, 0:8].unsqueeze(2).to_broadcast([P, 8, HD]), ALU.mult))
                    p.link(TT(ysum[:, t, :], ysum[:, t, :], ps[:, t, :], ALU.add))
                p.settle()

                def weigh(u):
                    d, s, t, _ = updates[u]
                    p.sig(TT(heads(mt[:, u % 2, :]), heads(xsn[:, t, :]), per_head(wst, t, d), ALU.mult), "xw_ready")

                def add_state(u):
                    d, t = updates[u][0], updates[u][3]
                    if t < tiles:
                        p.after("yoff_psum")
                        p.sig(TT(heads(yo[:]), heads(ps[:, 6, :]), per_head(ecs, t, d), ALU.mult), "yoff_read")
                        p.own("yoff_read")
                        p.chain(TT(ysum[:, t, :], ysum[:, t, :], yo[:], ALU.add))

                weigh(0)
                weigh(1)
                for u, (d, s, t, _) in enumerate(updates):
                    new, old = mt[:, 2 + u % 2, :], mt[:, 3 - u % 2, :]
                    if s > 0:
                        p.own("state_ready")
                        p.chain(TT(heads(new), heads(old), per_head(etot, t, d), ALU.mult))
                    p.after("state_psum")
                    if s == 0:
                        p.sig(V.tensor_copy(new, ps[:, 5 + 2 * (u % 2), :]), "state_ready")
                    else:
                        p.sig(TT(new, new, ps[:, 5 + 2 * (u % 2), :], ALU.add), "state_ready")
                    if u + 2 < len(updates):
                        weigh(u + 2)
                    if u > 0:
                        add_state(u - 1)
                add_state(len(updates) - 1)
                for t in range(tiles):
                    ins = TT(ysum[:, t, :], ysum[:, t, :], zs[:, t, :], ALU.mult)
                p.sig(ins, "y_gated")
                p.own("y_gated")
                p.after("y_rms")
                for t in range(tiles):
                    ins = TS(ysum[:, t, :], ysum[:, t, :], st4[:, t:t + 1], None, ALU.mult)
                p.sig(ins, "y_normed")
                split_features(l, 0, V_SSDG, n)
                p.barrier()
                for t in range(4):
                    h0 = 0 if t < tiles else 8
                    p.chain(TT(qkn[:, h0 * HD:QKW], qk[:, t, h0 * HD:QKW], qk[:, t, h0 * HD:QKW], ALU.mult))
                    if h0:
                        V.memset(rs40[:, t, 0:8], 1.0)
                    p.link(V.tensor_reduce(out=rs40[:, t, h0:10], in_=heads(qkn[:, h0 * HD:QKW]), op=ALU.add, axis=AX_X))
                    p.settle()
                p.sig(V.memset(sm[:, 2, 15:16], 0.0), "head_ss")
                p.after("head_rms")
                for t in range(4):
                    h0 = 0 if t < tiles else 8
                    q3, k3 = heads(qk[:, t, h0 * HD:QKW]), heads(qk[:, t, 512:QKW])
                    p.chain(TT(q3, q3, rs40[:, t, h0:10].unsqueeze(2).to_broadcast([P, 10 - h0, HD]), ALU.mult))
                    if t < tiles:
                        q4 = heads(qk[:, t, 0:512])
                        p.link(TT(q4, q4, qkg[:, l, 0:1, :].to_broadcast([P, 8, HD]), ALU.mult))
                    p.chain(TT(k3, k3, qkg[:, l, 1:2, :].to_broadcast([P, 2, HD]), ALU.mult))
                    if t > 0:
                        p.after("heads_transposed")
                    dq = qkn[:, 0:512].rearrange("p (b j d) -> p j b d", j=2, d=HD)
                    sq_ = qk[:, t, 0:512].rearrange("p (j b d) -> p j b d", j=2, d=HD)
                    kn = heads(qkn[:, 512:QKW])
                    if t < 2:
                        cosine, sine = c_rope[:, 0, t:t + 1, :], c_rope[:, 1, t, :].rearrange("p (a w d) -> p a w d", w=2, d=16)
                        for j in range(2):
                            p.link(TT(dq[:, j], sq_[:, j], cosine.to_broadcast([P, 4, HD]), ALU.mult))
                        p.link(TT(kn, k3, cosine.to_broadcast([P, 2, HD]), ALU.mult))
                        src = qk[:, t, :].rearrange("p (h a w d) -> p h a w d", a=2, w=2, d=16)
                        dst = ropt[:].rearrange("p (h a w d) -> p h a w d", a=2, w=2, d=16)
                        for w in range(2):
                            for a in range(2):
                                p.link(TT(dst[:, :, a, w, :], src[:, :, a, 1 - w, :],
                                          sine[:, a:a + 1, w, :].to_broadcast([P, 10, 16]), ALU.mult))
                        p.settle()
                        rq = ropt[:, 0:512].rearrange("p (j b d) -> p j b d", j=2, d=HD)
                        for j in range(2):
                            TT(dq[:, j], dq[:, j], rq[:, j], ALU.add)
                        p.sig(TT(qkn[:, 512:QKW], qkn[:, 512:QKW], ropt[:, 512:QKW], ALU.add), "heads_ready")
                    else:
                        if t < tiles:
                            for j in range(2):
                                V.tensor_copy(dq[:, j], sq_[:, j])
                        p.sig(V.tensor_copy(qkn[:, 512:QKW], qk[:, t, 512:QKW]), "heads_ready")
                p.after("heads_transposed")
                for i in range(8 * tiles + 2):
                    if i < 8 * tiles:
                        t, u = i // 8, i % 8
                        c8 = (t % 2) * 8 + u
                        p.after("scores")
                        p.sig(V.tensor_reduce(out=sm[:, 0, c8:c8 + 1], in_=ps[:, i % 2, 0:T if t < 2 else L], op=ALU.max,
                                              axis=AX_X, negate=True), "row_max")
                    if 1 <= i <= 8 * tiles:
                        keys = T if (i - 1) // 8 < 2 else L
                        p.after("probT_psum")
                        if i >= 3:
                            p.after("pv_done")
                        p.sig(V.tensor_copy(probT[:, (i - 1) % 2, 0:keys], ps[:, 2 + (i - 1) % 2, 0:keys]), "probT_ready")
                    if i >= 9 and (i - 1) % 8 == 0 or i == 8 * tiles + 1:
                        t = (i - 2) // 8 if i == 8 * tiles + 1 else (i - 9) // 8
                        if i == 8 * tiles + 1 or t < tiles - 1:
                            dve.wait_ge(S["pv_done"], PV_BEFORE[l] + 8 * (t + 1))
                            dve.wait_ge(S["probs_ready"], PV_BEFORE[l] + 8 * (t + 1))
                            s8 = slice((t % 2) * 8, (t % 2) * 8 + 8)
                            p.chain(V.reciprocal(sm[:, 2, s8], sm[:, 1, s8]))
                            rec = sm[:, 2, s8].rearrange("p (b j) -> p j b", j=2)
                            o4 = onat[:, t, :].rearrange("p (j b d) -> p j b d", j=2, d=HD)
                            v4 = ps[:, 6 + t % 2, :].rearrange("p (j b d) -> p j b d", j=2, d=HD)
                            for j in range(2):
                                ins = TT(o4[:, j], v4[:, j], rec[:, j, :].unsqueeze(2).to_broadcast([P, 4, HD]), ALU.mult)
                            p.sig(ins, "o_ready")
                p.after("pv_done", 2)
                p.own("o_ready")
                p.after("o_rms")
                for t in range(tiles):
                    ins = TS(onat[:, t, :], onat[:, t, :], st4[:, t:t + 1], None, ALU.mult)
                p.sig(ins, "o_normed")
                split_features(l, 4, V_ATTG, n)
                p.barrier()
                for s in range(n // L):
                    p.after("spec_psum")
                    for f in range(2):
                        kr, kim, kr2 = spec[:, f, :], spec[:, 2 + f, :], spec[:, 4 if f == 0 else 1, :]
                        uc, us = ps[:, f, :], ps[:, 2 + f, :]
                        p.link(TT(prod[:, 0, :], us, kim, ALU.mult))
                        p.link(TT(prod[:, 1, :], us, kr2, ALU.mult))
                        p.link(TT(yspec[:, f, :], uc, kr, ALU.mult))
                        p.link(TT(yspec[:, 2 + f, :], uc, kim, ALU.mult))
                        p.settle()
                        p.link(TT(yspec[:, f, :], yspec[:, f, :], prod[:, 0, :], ALU.subtract))
                        ins = TT(yspec[:, 2 + f, :], yspec[:, 2 + f, :], prod[:, 1, :], ALU.add)
                        if f == 0:
                            p.chain(ins)
                    p.sig(ins, "yspec_ready")
                    p.after("conv_psum")
                    for cb in range(4):
                        ins = TT(yhy[:, cb, s * L:(s + 1) * L], ps[:, CONV_BANK[cb], 0:L], x0[:, cb, s * L:(s + 1) * L], ALU.mult)
                    p.sig(ins, "yhy_part")
                p.own("yhy_part")
                p.after("hy_rms")
                for k in range(4):
                    p.sig(TT(yhy[:, k, 0:n], yhy[:, k, 0:n], hrs[:, 0:n], ALU.mult), "yhy_normed")
                p.own("yhy_normed")
                for k in range(4):
                    p.after("f_hi_ready")
                    STT(out=f_lo[:, 8 + k, 0:n], in0=yhy[:, k, 0:n], scalar=vecT[:, l, V_HYG + k:V_HYG + k + 1],
                        in1=f_hi[:, 8 + k, 0:n].bitcast(F32), op0=ALU.mult, op1=ALU.subtract)
                p.barrier()
                if l == 0:
                    dve.wait_ge(mod_done, MODB // 2)
                    read_mod(0, 16, MODB)
                    scale_mod(0, 1)
                residual(l, "out", 16, n)
                p.barrier()
                normed(n)
                for part, (c0, cnt) in enumerate(FFN):
                    g0, q0 = PLAN[l, f"gu{part}"]
                    bu = 2 * ((q0 + 1) % 2)
                    f0 = ffn_at(l, part)
                    with dve.Fori(0, cnt) as i:
                        split_w(g0 + 2, i * 2)
                        dve.wait_ge(pair_free[q0 % 2], i + (q0 // 2 + 1))
                        dve.wait_ge(w_used, i * 2 + (g0 + 2))
                        TT(hidden[:, :, 0:n], gate[:, :, 0:n], ps[:, bu:bu + 2, 0:n], ALU.mult).then_inc(pair_free[(q0 + 1) % 2], 1)
                        split_w(g0 + 3, i * 2)
                        dve.wait_ge(pair_free[(q0 + 1) % 2], i + ((q0 + 1) // 2 + 1))
                        dve.wait_ge(ffn_hi, i + (f0 + 1))
                        TT(f_lo[:, bass.ds(i * 2, 2), 0:n], hidden[:, :, 0:n],
                           f_hi[:, bass.ds(i * 2, 2), 0:n].bitcast(F32), ALU.subtract).then_inc(ffn_lo, 1)
                        dve.wait_ge(ffn_lo, i + (f0 + 1))
                    residual(l, f"down{part}", 40, n)
                p.barrier()
            p.after("rstd_ready")
            for k in range(KD):
                p.chain(TT(hf[:, k % 2, 0:L], xT[:, k, 0:L], rstd[:, 0:L], ALU.mult))
                p.sig(TS(y_fin[:, k, :], hf[:, k % 2, 0:L], vecT[:, 0, V_FIN + k:V_FIN + k + 1], None, ALU.mult), "y_fin_ready")
            p.after("y_fin_psum", KD)
            for t in range(2):
                for j in range(2):
                    ins = V.tensor_copy(y_nat[:, t, j * 512:(j + 1) * 512], ps[:, 2 * j + t, :])
            p.sig(ins, "y_nat_ready")


_INS = ["x", "c", "ctx", "c_ctx", "w_mod", "b_mod", "norm1_g", "w_in", "ssd_conv_w", "ssd_conv_b", "ssd_a_log",
        "ssd_dt_bias", "ssd_d", "ssd_norm_g", "q_norm_g", "k_norm_g", "attn_norm_g", "hy_conv_w", "hy_conv_b",
        "hy_w1", "hy_b1", "hy_freq", "hy_w2", "hy_b2", "hy_w3", "hy_bias", "hy_norm_g", "w_out", "norm2_g", "w_gu",
        "w_down", "final_g"]
_CONSTS = ["sq", "fwd", "inv", "feats", "decay", "rope"]


def kernel(**inputs):
    import concourse.bacc as bacc
    from concourse.bass_utils import run_bass_kernel_spmd

    nc = bacc.Bacc("TRN2", target_bir_lowering=False, num_devices=1)
    arrays, args = {}, []
    tables = constants()
    for name, a in [(n, inputs[n]) for n in _INS] + [(f"const_{n}", tables[n].astype(np.float32)) for n in _CONSTS]:
        a = np.ascontiguousarray(a)
        arrays[f"in_{name}_dram"] = a
        args.append(nc.dram_tensor(f"in_{name}_dram", a.shape, mybir.dt.from_np(a.dtype), kind="ExternalInput").ap())
    args.append(nc.dram_tensor("out_0_dram", (1, L, D), F32, kind="ExternalOutput").ap())
    backbone(nc, *args)
    r = run_bass_kernel_spmd(nc, [arrays], core_ids=[0])
    return r.results[0]["out_0_dram"]
```
